# Optimizing a Trainium2 kernel written in Bass

```python
import jax, jax.numpy as jnp
from jax import lax
import numpy as np

D_MODEL = 1024
BATCH = 1
SEQ = 1024
DEPTH = 1

CHUNK = 64
EPS = 1e-6

GLA_HEADS = 4
GLA_DK = 128
GLA_DV = 256
GLA_RANK = 16
GLA_TAU = 16.0
GLA_QK = GLA_HEADS * GLA_DK
GLA_V = GLA_HEADS * GLA_DV

SWA_HEADS = 16
SWA_KV_HEADS = 4
SWA_GROUP = SWA_HEADS // SWA_KV_HEADS
SWA_HD = 64
WINDOW = 128
WIN_CHUNKS = WINDOW // CHUNK
SWA_Q = SWA_HEADS * SWA_HD
SWA_KV = SWA_KV_HEADS * SWA_HD

D_FF = 4 * D_MODEL

IN_SIZES = (GLA_QK, GLA_QK, GLA_V, GLA_V, GLA_RANK, SWA_Q, SWA_KV, SWA_KV, D_MODEL, D_MODEL)
D_IN = sum(IN_SIZES)

kernel_name = "hybrid_gla_swa_gated_block"

def rmsnorm(x, g):
    xf = x.astype(jnp.float32)
    y = xf * lax.rsqrt(jnp.mean(xf * xf, axis=-1, keepdims=True) + EPS)
    return (y * g.astype(jnp.float32)).astype(x.dtype)

def gla_branch(q, k, v, g, a_lr, w_alpha2, b_alpha, gla_norm):
    f32 = jnp.float32
    B, T, _ = q.shape
    NC = T // CHUNK
    kshape = (B, NC, CHUNK, GLA_HEADS, GLA_DK)
    log_alpha = jax.nn.log_sigmoid((a_lr.astype(f32) @ w_alpha2.astype(f32)) + b_alpha.astype(f32)) / GLA_TAU
    cum = jnp.cumsum(log_alpha.reshape(kshape), axis=2)
    qf = q.astype(f32).reshape(kshape) * (GLA_DK ** -0.5)
    kf = k.astype(f32).reshape(kshape)
    vf = v.astype(f32).reshape(B, NC, CHUNK, GLA_HEADS, GLA_DV)
    q_dec = qf * jnp.exp(cum)
    k_dec = kf * jnp.exp(-cum)
    total = cum[:, :, -1]
    k_to_end = kf * jnp.exp(total[:, :, None] - cum)
    scores = jnp.einsum('bnthk,bnshk->bnhts', q_dec, k_dec)
    causal = jnp.tril(jnp.ones((CHUNK, CHUNK), dtype=bool))
    scores = jnp.where(causal, scores, 0.0)
    o_intra = jnp.einsum('bnhts,bnshv->bnthv', scores, vf)
    chunk_kv = jnp.einsum('bnshk,bnshv->bnhkv', k_to_end, vf)

    def step(state, inp):
        decay, kv = inp
        return state * jnp.exp(decay)[..., None] + kv, state

    init = jnp.zeros((B, GLA_HEADS, GLA_DK, GLA_DV), f32)
    _, states = lax.scan(step, init, (jnp.moveaxis(total, 1, 0), jnp.moveaxis(chunk_kv, 1, 0)))
    states = jnp.moveaxis(states, 0, 1)
    o = o_intra + jnp.einsum('bnthk,bnhkv->bnthv', q_dec, states)
    o = o * lax.rsqrt(jnp.mean(o * o, axis=-1, keepdims=True) + EPS) * gla_norm.astype(f32)
    o = o.reshape(B, T, GLA_V) * jax.nn.silu(g.astype(f32))
    return o.astype(q.dtype)

def swa_branch(q, k, v, q_norm, k_norm, sinks):
    f32 = jnp.float32
    B, T, _ = q.shape
    NC = T // CHUNK
    S = (WIN_CHUNKS + 1) * CHUNK
    qh = rmsnorm(q.reshape(B, T, SWA_HEADS, SWA_HD), q_norm)
    kh = rmsnorm(k.reshape(B, T, SWA_KV_HEADS, SWA_HD), k_norm)
    vh = v.reshape(B, T, SWA_KV_HEADS, SWA_HD)
    pad = ((0, 0), (WIN_CHUNKS * CHUNK, 0), (0, 0), (0, 0))
    kc = jnp.pad(kh, pad).reshape(B, NC + WIN_CHUNKS, CHUNK, SWA_KV_HEADS, SWA_HD)
    vc = jnp.pad(vh, pad).reshape(B, NC + WIN_CHUNKS, CHUNK, SWA_KV_HEADS, SWA_HD)
    k_band = jnp.concatenate([kc[:, j:j + NC] for j in range(WIN_CHUNKS + 1)], axis=2)
    v_band = jnp.concatenate([vc[:, j:j + NC] for j in range(WIN_CHUNKS + 1)], axis=2)
    qg = qh.reshape(B, NC, CHUNK, SWA_KV_HEADS, SWA_GROUP, SWA_HD)
    scores = jnp.einsum('bnqkgd,bnskd->bnkgqs', qg, k_band).astype(f32) * (SWA_HD ** -0.5)
    slopes = (2.0 ** (-8.0 * jnp.arange(1, SWA_HEADS + 1, dtype=f32) / SWA_HEADS)).reshape(SWA_KV_HEADS, SWA_GROUP, 1, 1)
    dist = jnp.abs(jnp.arange(CHUNK)[:, None] + WIN_CHUNKS * CHUNK - jnp.arange(S)[None, :]).astype(f32)
    scores = scores - slopes * dist
    key_chunk = jnp.arange(NC)[:, None] - WIN_CHUNKS + (jnp.arange(S) // CHUNK)[None, :]
    valid = key_chunk >= 0
    scores = jnp.where(valid[None, :, None, None, None, :], scores, -1e30)
    sink = sinks.astype(f32).reshape(SWA_KV_HEADS, SWA_GROUP, 1, 1)
    m = jnp.maximum(jnp.max(scores, axis=-1, keepdims=True), sink)
    p = jnp.exp(scores - m)
    probs = p / (jnp.sum(p, axis=-1, keepdims=True) + jnp.exp(sink - m))
    o = jnp.einsum('bnkgqs,bnskd->bnqkgd', probs, v_band.astype(f32))
    return o.reshape(B, T, SWA_Q).astype(q.dtype)

def setup_inputs(seed: int = 0) -> dict:
    key = jax.random.key(seed)
    ks = jax.random.split(key, 16)
    f32 = jnp.float32
    L = DEPTH

    def nrm(k, shape, scale):
        return jax.random.normal(k, shape, f32) * scale

    return {
        "x": jax.random.normal(ks[0], (BATCH, SEQ, D_MODEL), f32),
        "norm_mix": 1.0 + nrm(ks[1], (L, D_MODEL), 0.02),
        "w_in": nrm(ks[2], (L, D_MODEL, D_IN), D_MODEL ** -0.5),
        "w_alpha2": nrm(ks[3], (L, GLA_RANK, GLA_QK), GLA_RANK ** -0.5),
        "b_alpha": nrm(ks[4], (L, GLA_QK), 0.1),
        "gla_norm": 1.0 + nrm(ks[5], (L, GLA_DV), 0.02),
        "swa_q_norm": 1.0 + nrm(ks[6], (L, SWA_HD), 0.02),
        "swa_k_norm": 1.0 + nrm(ks[7], (L, SWA_HD), 0.02),
        "swa_sinks": nrm(ks[8], (L, SWA_HEADS), 0.5),
        "w_branch_gla": nrm(ks[9], (L, GLA_V, D_MODEL), GLA_V ** -0.5),
        "w_branch_swa": nrm(ks[10], (L, SWA_Q, D_MODEL), SWA_Q ** -0.5),
        "w_out": nrm(ks[11], (L, D_MODEL, D_MODEL), D_MODEL ** -0.5),
        "norm_mlp": 1.0 + nrm(ks[12], (L, D_MODEL), 0.02),
        "w_up": nrm(ks[13], (L, D_MODEL, D_FF), D_MODEL ** -0.5),
        "w_down": nrm(ks[14], (L, D_FF, D_MODEL), D_FF ** -0.5),
    }

def reference(x, norm_mix, w_in, w_alpha2, b_alpha, gla_norm, swa_q_norm, swa_k_norm, swa_sinks,
              w_branch_gla, w_branch_swa, w_out, norm_mlp, w_up, w_down):
    h = x
    split_at = np.cumsum(IN_SIZES)[:-1].tolist()
    for l in range(DEPTH):
        hn = rmsnorm(h, norm_mix[l])
        proj = hn @ w_in[l]
        (gq, gk, gv, gg, ga, sq, sk, sv, gate_a, gate_b) = jnp.split(proj, split_at, axis=-1)
        y_gla = gla_branch(gq, gk, gv, gg, ga, w_alpha2[l], b_alpha[l], gla_norm[l]) @ w_branch_gla[l]
        y_swa = swa_branch(sq, sk, sv, swa_q_norm[l], swa_k_norm[l], swa_sinks[l]) @ w_branch_swa[l]
        merged = jax.nn.sigmoid(gate_a) * y_gla + jax.nn.sigmoid(gate_b) * y_swa
        h = h + (merged @ w_out[l]).astype(h.dtype)
        hm = rmsnorm(h, norm_mlp[l])
        u = jnp.square(jax.nn.relu(hm @ w_up[l]))
        h = h + (u @ w_down[l]).astype(h.dtype)
    return h


_drawn_inputs = setup_inputs


def setup_inputs(seed=0):
    import zlib

    import numpy as np

    out = dict(_drawn_inputs(seed))
    spreads = {}
    factors = {'norm_mix': 3.586,
     'b_alpha': 3.801,
     'gla_norm': 8.0,
     'swa_q_norm': 8.0,
     'swa_k_norm': 8.0,
     'swa_sinks': 8.0,
     'norm_mlp': 11.442}
    for name, (base, spread) in spreads.items():
        noise = np.random.default_rng([zlib.crc32(name.encode()), seed]).standard_normal(out[name].shape)
        drawn = base * np.exp(spread * noise) if base else spread * noise
        out[name] = __import__('jax').numpy.asarray(drawn.astype(out[name].dtype))
    for name, factor in factors.items():
        out[name] = (out[name] * factor).astype(out[name].dtype)
    return out
```

```python
from contextlib import ExitStack

import concourse.bass as bass
from concourse import mybir

F32 = mybir.dt.float32
F32R = mybir.dt.float32r
I32 = mybir.dt.int32
ALU = mybir.AluOpType
ACT = mybir.ActivationFunctionType
AX_X = mybir.AxisListType.X

P = 128
EPS = 1e-6
NEG = -1e30
D_MODEL = 1024
SEQ = 1024
HALVES = 2
POOL_CONSTS = 19
CONST_DMAS = 11
T = SEQ // HALVES
TT = T // P
KB = D_MODEL // P
CHUNK = 64
NCH = T // CHUNK
GLA_HEADS, DK, DV, RANK = 4, 128, 256, 16
GLA_TAU = 16.0
SWA_HEADS, KV_HEADS, HD = 16, 4, 64
PAIRS = KV_HEADS // 2
PAIR_HEADS = SWA_HEADS // PAIRS
UNITS = TT * 2
D_FF = 4 * D_MODEL

GQ = 0
GK = GQ + GLA_HEADS * DK
GV = GK + GLA_HEADS * DK
GG = GV + GLA_HEADS * DV
GA = GG + GLA_HEADS * DV
SQ = GA + RANK
SK = SQ + SWA_HEADS * HD
SV = SK + KV_HEADS * HD
GATE_A = SV + KV_HEADS * HD
GATE_B = GATE_A + D_MODEL

HEAD_TILES = 6
N_GLA = 0
N_GATE_A = N_GLA + GLA_HEADS * HEAD_TILES
N_BRANCH_A = N_GATE_A + KB
N_SWA = N_BRANCH_A + KB
N_GATE_B = N_SWA + PAIRS * HEAD_TILES
N_BRANCH_B = N_GATE_B + KB
N_OUT = N_BRANCH_B + KB
N_MLP = N_OUT + KB
QUERY_TILES = [N_SWA + p * HEAD_TILES + t for p in range(PAIRS) for t in range(2, HEAD_TILES)]
MLP_TURNS = 4
TURN_TILES = 2 * KB
TILES = N_MLP + MLP_TURNS * TURN_TILES
WSLOTS = 4
RSLOTS = 2
AHEAD = 3
DBANKS = 2

LN_EXP = "natural_log_exp_and_others"
C_MIX, C_MLP, C_BA, C_GN, C_QN, C_KN, C_ALL = 0, 8, 16, 20, 22, 23, 24


class Stream:

    def __init__(self, sem, credit=1, **steps):
        self.sem, self.credit, self.ends, self.sizes, n = sem, credit, {}, steps, 0
        for name, size in steps.items():
            self.ends[name] = n
            n += size
        self.size = n

    def at(self, turn, step, nth=None):
        last = self.sizes[step] if nth is None else nth + 1
        return turn * self.size + (self.credit * self.size + self.ends[step] + last)

    def start(self, eng):
        eng.sem_inc(self.sem, self.credit * self.size)


def program(nc, x, norm_mix, w_in, w_alpha2, b_alpha, gla_norm, swa_q_norm, swa_k_norm, swa_sinks,
            w_branch_gla, w_branch_swa, w_out, norm_mlp, w_up, w_down, out):
    with ExitStack() as ctx:
        def sb(name, shape, dt=F32, stack=ctx):
            return stack.enter_context(nc.sbuf_tensor(name, shape, dt))

        def sem(name):
            return ctx.enter_context(nc.semaphore(name))

        def stream(name, credit=1, **steps):
            return Stream(sem(name), credit, **steps)

        resid = sb("resid", [P, KB, T])
        gate = sb("gate", [P, KB, T])
        x_tok = gate[:].rearrange("p (t a) c -> p t (a c)", t=TT)
        act_x = [sb("act_x_hi", [P, KB, T], F32R), sb("act_x_lo", [P, KB, T], F32R)]
        act_o = [sb("act_o_hi", [P, KB, T], F32R), sb("act_o_lo", [P, KB, T], F32R)]
        w_raw = sb("w_raw", [P, RSLOTS, KB, P])
        w_hi = sb("w_hi", [P, WSLOTS, KB, P], F32R)
        w_lo = sb("w_lo", [P, WSLOTS, KB, P], F32R)

        ident = sb("ident", [P, P])
        ones = sb("ones", [P, P])
        ones_hd = sb("ones_hd", [P, P])
        causal = sb("causal", [P, P], I32)
        restart = sb("restart", [P, P])
        dist = sb("dist", [P, 2 * P])
        eps = sb("eps", [P, 1])
        cols = sb("cols", [P, C_ALL])
        sink_row = sb("sink_row", [1, SWA_HEADS])
        sink = sb("sink", [P, SWA_HEADS])
        w_a2 = sb("w_a2", [RANK, GLA_HEADS * DK])
        wa_hi = sb("wa_hi", [P, KB * RANK + P], F32R)
        wa_lo = sb("wa_lo", [P, KB * RANK + P], F32R)
        a_low = sb("a_low", [RANK, T])
        no_past = sb("no_past", [P, 1])
        carry = sb("carry", [P, GLA_HEADS, DV])
        masked = sb("masked", [P, TT, P])
        k_win = sb("k_win", [P, PAIRS, P + T])
        v_win = sb("v_win", [P, PAIRS, 1 + TT, P])
        sq_ring = sb("sq_ring", [P, 2, T])
        o_stage = sq_ring[:].rearrange("p s (t c) -> p s t c", t=TT)

        with ExitStack() as region:
            causal_f = sb("causal_f", [P, P], F32, region)
            rows = sb("rows", [C_ALL, P], F32, region)
            wa_raw = sb("wa_raw", [P, KB * RANK + P], F32, region)
        with ExitStack() as region:
            vT = sb("vT", [P, T], F32, region)
            v_tok = sb("v_tok", [P, TT, DV], F32, region)
            silu = sb("silu", [P, 2, 2, T], F32, region)
            t_a = sb("t_a", [P, T], F32, region)
            t_b = sb("t_b", [P, T], F32, region)
            cum = sb("cum", [P, T], F32, region)
            decay = sb("decay", [P, 2, NCH], F32, region)
            q_dec = sb("q_dec", [P, T], F32, region)
            k_dec = sb("k_dec", [P, T], F32, region)
            k_end = sb("k_end", [P, T], F32, region)
            ke_tok = sb("ke_tok", [P, TT, P], F32, region)
            state = sb("state", [P, NCH, DV], F32, region)
            o_tok = sb("o_tok", [P, TT, DV], F32, region)
            o_ss = sb("o_ss", [P, TT], F32, region)
            o_rs = sb("o_rs", [P, TT], F32, region)
        with ExitStack() as region:
            qT = sb("qT", [P, 4, T], F32, region)
            qk_raw = sb("qk_raw", [P, 2, T], F32, region)
            svT = sb("svT", [P, T], F32, region)
            bias = sb("bias", [P, PAIR_HEADS, 2 * P], F32, region)
            prob = sb("prob", [P, 2, 4, 2 * P], F32, region)
            probT = sb("probT", [P, 4, 2, P], F32, region)
            s_tok = sb("s_tok", [P, 2, 8, HD], F32, region)
            s_sink = sb("s_sink", [P, 2, 4], F32, region)
            mx = sb("mx", [P, 2, 4], F32, region)
            m_all = sb("m_all", [P, 2, 4], F32, region)
            m_neg = sb("m_neg", [P, 2, 4], F32, region)
            s_gap = sb("s_gap", [P, 2, 4], F32, region)
            s_exp = sb("s_exp", [P, 2, 4], F32, region)
            den = sb("den", [P, 2, 8], F32, region)
            den_all = sb("den_all", [P, 2, 4], F32, region)
            den_inv = sb("den_inv", [P, 2, 8], F32, region)
        with ExitStack() as region:
            act_m = [sb("act_m_hi", [P, KB, T], F32R, region), sb("act_m_lo", [P, KB, T], F32R, region)]
            sq_sum = sb("sq_sum", [P, T], F32, region)
            rs_mlp = sb("rs_mlp", [P, T], F32, region)
        with ExitStack() as region:
            relu = sb("relu", [P, 2, T], F32, region)
            x_sq = sb("x_sq", [P, D_MODEL], F32, region)
            x_diag = sb("x_diag", [P, TT, P], F32, region)
            x_ss = sb("x_ss", [P, TT], F32, region)
            x_rs = sb("x_rs", [P, TT], F32, region)

        bank = [ctx.enter_context(nc.psum_tensor(f"bank{i}", [P, T], F32)) for i in range(8)]
        by_tt = [b[:].rearrange("p (t c) -> p t c", t=TT) for b in bank]
        by_dv = [b[:].rearrange("p (t c) -> p t c", c=DV) for b in bank]

        const_dma = sem("const_dma")
        const_pool = sem("const_pool")
        const_done = sem("const_done")
        cols_pe = sem("cols_pe")
        cols_dve = sem("cols_dve")
        raw_loaded = [sem(f"raw_loaded{i}") for i in range(RSLOTS)]
        side_loaded = [sem(f"side_loaded{i}") for i in range(RSLOTS)]
        w_hi_done = stream("w_hi_done", 0, w=1)
        w_lo_done = stream("w_lo_done", RSLOTS, w=1)
        tile_done = stream("tile_done", WSLOTS, t=1)
        evac = [stream(f"evac{i}", TILES // DBANKS, t=1) for i in range(DBANKS)]
        x_loaded = [sem(f"x_loaded{t}") for t in range(TT)]
        res_loaded = [sem(f"res_loaded{i}") for i in range(2)]
        stored = [sem(f"stored{i}") for i in range(2)]
        xn_stat = stream("xn_stat", 1, ss=TT, ln=1, rs=1)
        xn_diag = stream("xn_diag", 1, d=TT)
        xn_pe = stream("xn_pe", 1, t=KB)
        xn_hi = stream("xn_hi", 1, h=KB)
        xn_lo = stream("xn_lo", 1, l=KB)
        res_pe = stream("res_pe", 1, t=KB)
        res_copy = stream("res_copy", 1, c=KB)
        hm_hi = stream("hm_hi", 1, h=KB)
        hm_sq = stream("hm_sq", 1, s=KB)
        hm_lo = stream("hm_lo", 1, l=KB)
        hm_add = stream("hm_add", 1, a=KB - 1)
        hm_sum = stream("hm_sum", 1, s=1)
        hm_rs = stream("hm_rs", 1, ln=1, rs=1)
        shifted = stream("shifted", 1, k=1, v=1)
        lr_pe = stream("lr_pe", 1, t=1)
        lr_copy = stream("lr_copy", 1, t=1)
        al_pe = stream("al_pe", 1, z=1)
        al_act = stream("al_act", 1, abs=1, exp=1, ln=1)
        al_exp = stream("al_exp", 1, dec=1, e1=1, e3=1, e2=1)
        al_dve = stream("al_dve", 1, zmin=1, la=1, scan=TT, gap=1)
        v_pe = stream("v_pe", 1, t=2)
        v_copy = stream("v_copy", 1, t=2)
        g_tanh = stream("g_tanh", 1, t=2)
        ga_pe = stream("ga_pe", 1, ke=1, sc=1, kv=4, o=2, ot=2)
        ga_dve = stream("ga_dve", GLA_HEADS, ke=1, first=1, mask=TT, st=NCH, f=2)
        ga_lo = stream("ga_lo", 1, lo=2)
        ga_act = stream("ga_act", 1, ss=TT, ln=1, rs=1, o=TT, hi=2)
        sn_act = stream("sn_act", 1, sq=1, ln=1, rs=1)
        sn_pe = stream("sn_pe", 1, s=1)
        sn_dve = stream("sn_dve", 1, n=1)
        sv_pe = stream("sv_pe", 1, t=1)
        sv_copy = stream("sv_copy", 1, t=1)
        past_dve = stream("past_dve", 1, off=1)
        bias_act = stream("bias_act", 1, b=PAIR_HEADS, again=PAIR_HEADS)
        bias_dve = stream("bias_dve", 1, past=1)
        sc_pe = stream("sc_pe", 1, s=1)
        sm_dve = stream("sm_dve", 1, sinks=1, ttr=4, m=1, neg=1, gap=1)
        sm_act = stream("sm_act", 1, p=4, sink=1)
        dn_dve = stream("dn_dve", 1, sum=1, inv=1)
        pt_pe = stream("pt_pe", 2, t=2)
        pt_dve = stream("pt_dve", 1, c=1)
        pt_act = stream("pt_act", 1, c=1)
        pv_pe = stream("pv_pe", 1, o=1)
        so_dve = stream("so_dve", 1, o=1)
        so_pe = stream("so_pe", 1, t=1)
        so_hi = stream("so_hi", 1, h=1)
        so_lo = stream("so_lo", 1, l=1)
        mg_dve = stream("mg_dve", 1, mul=1, add=1)
        mg_act = stream("mg_act", 1, hi=1)
        up_relu = stream("up_relu", 1, r=1)
        up_sq = stream("up_sq", 1, sq=1, hi=1)
        fin_pe = stream("fin_pe", 1, t=KB)
        fin_act = stream("fin_act", 1, c=KB)

        def left(half, n, turn=0):
            return evac[n % DBANKS].at(half * (TILES // DBANKS) + turn * (TURN_TILES // DBANKS) + n // DBANKS, "t")

        def x_rows(half):
            return (x[0].rearrange("(h t p) d -> h p t d", h=HALVES, p=P)[bass.ds(half, 1)]
                    .rearrange("h p t d -> p (h t) d"))

        swa_round = lambda half, p: half * PAIRS + p
        qk_round = lambda half, p, t: half * (PAIRS * 5) + (p * 5 + t)
        unit_round = lambda half, p, u: half * (PAIRS * UNITS) + (p * UNITS + u)
        block_round = lambda half, p, b: half * (PAIRS * TT) + (p * TT + b)
        gla_round = lambda half, h: half * GLA_HEADS + h
        up_round = lambda half, turn, j: half * (MLP_TURNS * KB) + turn * KB + j
        slopes = [2.0 ** (-8.0 * (h + 1) / SWA_HEADS) for h in range(SWA_HEADS)]

        w_in_v = w_in[0].rearrange("(k p) n -> p k n", p=P)
        block = ctx.enter_context(nc.Block())

        @block.sync
        def _(sp):
            def load(N, n, src):
                sp.wait_ge(w_lo_done.sem, w_lo_done.at(N - RSLOTS, "w"))
                if isinstance(src, list):
                    sp.dma_start(w_raw[:, n % RSLOTS, :, 0:HD], src[0]).then_inc(side_loaded[n % RSLOTS], 16)
                    sp.dma_start(w_raw[:, n % RSLOTS, :, HD:], src[1]).then_inc(raw_loaded[n % RSLOTS], 16)
                else:
                    sp.dma_start(w_raw[:, n % RSLOTS], src).then_inc(raw_loaded[n % RSLOTS], 16)

            def matrix(w, c):
                return w[0].rearrange("(k p) n -> p k n", p=P)[:, :, c * P:(c + 1) * P]

            for t in range(TT):
                sp.dma_start(x_tok[:, t:t + 1], x_rows(0)[:, t:t + 1]).then_inc(x_loaded[t], 16)
            with nc.sync.Fori(0, HALVES) as half:
                N = half * TILES
                cols_of = []
                for h in range(GLA_HEADS):
                    cols_of += [GG + h * DV, GG + h * DV + P, GV + h * DV, GV + h * DV + P, GQ + h * DK, GK + h * DK]
                for j, c in enumerate(cols_of):
                    load(N + j, j, w_in_v[:, :, c:c + P])
                for c in range(KB):
                    load(N + N_GATE_A + c, N_GATE_A + c, w_in_v[:, :, GATE_A + c * P:GATE_A + (c + 1) * P])
                for c in range(KB):
                    load(N + N_BRANCH_A + c, N_BRANCH_A + c, matrix(w_branch_gla, c))
                n = N_SWA
                for p in range(PAIRS):
                    for c in (SK + p * P, SV + p * P):
                        load(N + n, n, w_in_v[:, :, c:c + P])
                        n += 1
                    for j in range(4):
                        c = SQ + (p * PAIR_HEADS + j) * HD
                        d = c + PAIR_HEADS // 2 * HD
                        load(N + n, n, [w_in_v[:, :, c:c + HD], w_in_v[:, :, d:d + HD]])
                        n += 1
                for c in range(KB):
                    load(N + N_GATE_B + c, N_GATE_B + c, w_in_v[:, :, GATE_B + c * P:GATE_B + (c + 1) * P])
                for c in range(KB):
                    load(N + N_BRANCH_B + c, N_BRANCH_B + c, matrix(w_branch_swa, c))
                for c in range(KB):
                    load(N + N_OUT + c, N_OUT + c, matrix(w_out, c))
                up_v = w_up[0].rearrange("(k p) n -> p k n", p=P)
                down_v = w_down[0].rearrange("(g k p) n -> g p k n", p=P, k=KB)

                def load_up(j, n, turn, up_turn):
                    load(half * TILES + turn * TURN_TILES + n, n,
                         up_v[:, :, bass.ds(up_turn * (KB * P) + j * P, P)])

                def load_down(c, n, turn):
                    w = down_v[bass.ds(turn, 1), :, :, c * P:(c + 1) * P]
                    load(half * TILES + turn * TURN_TILES + n, n, w.rearrange("g p k n -> p (g k) n"))

                for j in range(KB):
                    load_up(j, N_MLP + j, 0, 0)
                with nc.sync.Fori(0, MLP_TURNS - 1) as turn:
                    for c in range(KB):
                        load_down(c, N_MLP + KB + c, turn)
                    for j in range(KB):
                        load_up(j, N_MLP + 2 * KB + j, turn, turn + 1)
                for c in range(KB):
                    load_down(c, N_MLP + KB + c, MLP_TURNS - 1)
            for s in stored:
                sp.wait_ge(s, 16 * HALVES * KB // 2 + 16)

        @block.gpsimd
        def _(pool):
            count = [0]

            def link(ins):
                ins.then_inc(const_pool, 1)
                count[0] += 1
                pool.wait_ge(const_pool, count[0])

            g = nc.gpsimd
            w_lo_done.start(pool)
            link(g.memset(ident[:], 0.0))
            link(g.affine_select(out=ident[:], in_=ident[:], compare_op=ALU.not_equal, fill=1.0, base=0,
                                 pattern=[[-1, P]], channel_multiplier=1))
            link(g.memset(ones[:], 1.0))
            link(g.memset(ones_hd[:], 0.0))
            link(g.memset(ones_hd[0:HD, 0:HD], 1.0))
            link(g.memset(ones_hd[HD:P, HD:P], 1.0))
            link(g.affine_select(out=causal_f[:], in_=ones_hd[:], compare_op=ALU.is_ge, fill=0.0, base=0,
                                 pattern=[[1, P]], channel_multiplier=-1))
            link(g.tensor_copy(causal[:], causal_f[:]))
            link(g.memset(restart[:], 1.0))
            link(g.memset(restart[:, 0:1], 0.0))
            link(g.memset(restart[:, CHUNK:CHUNK + 1], 0.0))
            link(g.iota(dist[:], pattern=[[1, 2 * P]], base=-P, channel_multiplier=-1,
                        allow_small_or_imprecise_dtypes=True))
            link(g.memset(eps[:], EPS))
            link(g.memset(no_past[:], NEG))
            link(g.memset(carry[:], 0.0))
            link(g.memset(masked[:], 0.0))
            link(g.memset(k_win[:], 0.0))
            link(g.memset(v_win[:], 0.0))
            link(g.memset(wa_raw[:, KB * RANK:], 0.0))
            assert count[0] == POOL_CONSTS
            with nc.gpsimd.Fori(0, HALVES * TILES // WSLOTS) as turn:
                for j in range(WSLOTS):
                    N = turn * WSLOTS + j
                    pool.wait_ge(w_hi_done.sem, w_hi_done.at(N, "w"))
                    g.tensor_tensor(w_lo[:, j], w_raw[:, j % RSLOTS], w_hi[:, j].bitcast(F32),
                                    ALU.subtract).then_inc(w_lo_done.sem, 1)

        @block.scalar
        def _(act):
            a = nc.scalar
            for s in ([xn_stat, xn_hi, res_copy, hm_hi, hm_sq, hm_rs, lr_copy, al_act, al_exp, g_tanh, ga_act, sn_act,
                                       bias_act, sm_act, pt_act, so_hi, mg_act, up_sq, fin_act]):
                s.start(act)
            for s in stored:
                act.sem_inc(s, 16)
            gain_rows = [(norm_mix, C_MIX, 8), (norm_mlp, C_MLP, 8), (b_alpha, C_BA, 4), (gla_norm, C_GN, 2)]
            for v, at, n in gain_rows:
                act.dma_start(rows[at:at + n, :], v[0].rearrange("(r c) -> r c", r=n)).then_inc(const_dma, 16)
            for v, at in ((swa_q_norm, C_QN), (swa_k_norm, C_KN)):
                for side in range(2):
                    act.dma_start(rows[at:at + 1, side * HD:(side + 1) * HD], v[0:1, :]).then_inc(const_dma, 16)
            act.dma_start(sink_row[:], swa_sinks[0:1, :]).then_inc(const_dma, 16)
            act.dma_start(w_a2[:], w_alpha2[0]).then_inc(const_dma, 16)
            act.dma_start(wa_raw[:, 0:KB * RANK].rearrange("p (k r) -> p k r", k=KB),
                         w_in_v[:, :, GA:GA + RANK]).then_inc(const_dma, 16)

            act.wait_ge(const_pool, POOL_CONSTS)
            act.wait_ge(const_dma, CONST_DMAS * 16)
            a.activation(dist[:], dist[:], ACT.Abs).then_inc(const_done, 1)
            act.wait_ge(const_done, 1)
            a.activation(dist[:], dist[:], ACT.Copy, scale=-1.0).then_inc(const_done, 1)
            a.activation(wa_hi[:], wa_raw[:], ACT.Copy).then_inc(const_done, 1)

            def high(half, n):
                N = half * TILES + n
                occurrence = half * (TILES // RSLOTS) + n // RSLOTS
                act.wait_ge(raw_loaded[n % RSLOTS], occurrence * 16 + 16)
                if n in QUERY_TILES:
                    before = [q for q in QUERY_TILES if q < n and q % RSLOTS == n % RSLOTS]
                    act.wait_ge(side_loaded[n % RSLOTS],
                                half * (len(QUERY_TILES) // RSLOTS * 16) + 16 * len(before) + 16)
                act.wait_ge(tile_done.sem, tile_done.at(N - WSLOTS, "t"))
                a.activation(w_hi[:, n % WSLOTS], w_raw[:, n % RSLOTS], ACT.Copy).then_inc(w_hi_done.sem, 1)

            def token_square(R, t):
                act.wait_ge(x_loaded[t], R * 16 + 16)
                if t > 0:
                    act.wait_ge(xn_stat.sem, xn_stat.at(R, "ss", t - 1))
                a.activation(x_sq[:], x_tok[:, t], ACT.Square, accum_out=x_ss[:, t:t + 1]).then_inc(xn_stat.sem, 1)

            def token_rs(R):
                act.wait_ge(xn_stat.sem, xn_stat.at(R, "ss"))
                a.activation(x_rs[:], x_ss[:], ACT.Ln, bias=eps[:], scale=1.0 / D_MODEL).then_inc(xn_stat.sem, 1)
                act.wait_ge(xn_stat.sem, xn_stat.at(R, "ln"))
                a.activation(x_rs[:], x_rs[:], ACT.Exp, scale=-0.5).then_inc(xn_stat.sem, 1)

            def x_high(R, k):
                act.wait_ge(xn_pe.sem, xn_pe.at(R, "t", k))
                a.activation(act_x[0][:, k], bank[4 + k % 4][:], ACT.Copy,
                             scale=cols[:, C_MIX + k:C_MIX + k + 1]).then_inc(xn_hi.sem, 1)

            a.preload_act_table_set(LN_EXP)
            for t in range(TT):
                token_square(0, t)
            token_rs(0)
            act.wait_ge(cols_dve, 5)
            for k in range(KB):
                x_high(0, k)

            with nc.scalar.Fori(0, HALVES) as half:
                for n in range(AHEAD):
                    high(half, n)
                act.wait_ge(lr_pe.sem, lr_pe.at(half, "t"))
                a.activation(a_low[:], bank[2][0:RANK, :], ACT.Copy).then_inc(lr_copy.sem, 1)

                def alpha_ln(h):
                    R = gla_round(half, h)
                    act.wait_ge(al_pe.sem, al_pe.at(R, "z"))
                    if h > 0:
                        act.wait_ge(evac[(HEAD_TILES * h - 1) % DBANKS].sem, left(half, HEAD_TILES * h - 1))
                    ba = cols[:, C_BA + h:C_BA + h + 1]
                    a.activation(t_a[:], bank[2][:], ACT.Abs, bias=ba).then_inc(al_act.sem, 1)
                    act.wait_ge(al_act.sem, al_act.at(R, "abs"))
                    a.activation(t_a[:], t_a[:], ACT.Exp, scale=-1.0).then_inc(al_act.sem, 1)
                    a.preload_act_table_set(LN_EXP)
                    act.wait_ge(al_act.sem, al_act.at(R, "exp"))
                    a.activation(t_a[:], t_a[:], ACT.Ln, bias=ones[:, 0:1]).then_inc(al_act.sem, 1)

                def alpha_exp(h):
                    R = gla_round(half, h)
                    act.wait_ge(al_dve.sem, al_dve.at(R, "scan"))
                    total = cum[:].rearrange("p (c s) -> p c s", s=CHUNK)[:, :, CHUNK - 1]
                    a.activation(decay[:, h % 2], total, ACT.Exp, scale=1.0 / GLA_TAU).then_inc(al_exp.sem, 1)
                    a.activation(t_a[:], cum[:], ACT.Exp, scale=1.0 / GLA_TAU).then_inc(al_exp.sem, 1)
                    act.wait_ge(al_dve.sem, al_dve.at(R, "gap"))
                    a.activation(t_b[:], t_b[:], ACT.Exp, scale=-1.0 / GLA_TAU).then_inc(al_exp.sem, 1)
                    act.wait_ge(al_exp.sem, al_exp.at(R, "e1"))
                    a.activation(cum[:], cum[:], ACT.Exp, scale=-1.0 / GLA_TAU).then_inc(al_exp.sem, 1)

                def v_out(h, j):
                    n = HEAD_TILES * h + 2 + j
                    act.wait_ge(tile_done.sem, tile_done.at(half * TILES + n, "t"))
                    act.wait_ge(v_pe.sem, v_pe.at(gla_round(half, h) + j - 1, "t", 1 - j))
                    a.activation(vT[:], bank[n % DBANKS][:], ACT.Copy).then_inc(evac[n % DBANKS].sem, 1)

                def g_out(h, j):
                    n = HEAD_TILES * h + j
                    act.wait_ge(tile_done.sem, tile_done.at(half * TILES + n, "t"))
                    a.activation(silu[:, h % 2, j], bank[n % DBANKS][:], ACT.Tanh, scale=0.5).then_inc(g_tanh.sem, 1)

                def gla_norm_out(g):
                    R = gla_round(half, g)
                    if g == 0:
                        for s in stored:
                            act.wait_ge(s, half * (16 * KB // 2) + 16)
                    for b in range(TT):
                        act.wait_ge(ga_pe.sem, ga_pe.at(R, "o", b // 2))
                        a.activation(sq_ring[:, b // 2, b % 2 * DV:b % 2 * DV + DV], by_dv[4 + b // 2][:, b % 2], ACT.Square,
                                     accum_out=o_ss[:, b:b + 1]).then_inc(ga_act.sem, 1)
                    a.preload_act_table_set(LN_EXP)
                    act.wait_ge(ga_act.sem, ga_act.at(R, "ss"))
                    a.activation(o_rs[:], o_ss[:], ACT.Ln, bias=eps[:], scale=1.0 / DV).then_inc(ga_act.sem, 1)
                    act.wait_ge(ga_act.sem, ga_act.at(R, "ln"))
                    a.activation(o_rs[:], o_rs[:], ACT.Exp, scale=-0.5).then_inc(ga_act.sem, 1)
                    act.wait_ge(ga_act.sem, ga_act.at(R, "rs"))
                    for b in range(TT):
                        a.activation(o_tok[:, b], by_dv[4 + b // 2][:, b % 2], ACT.Copy,
                                     scale=o_rs[:, b:b + 1]).then_inc(ga_act.sem, 1)

                def gla_high_out(g):
                    R = gla_round(half, g)
                    for j in range(2):
                        act.wait_ge(ga_dve.sem, ga_dve.at(R, "f", j))
                        a.activation(act_o[0][:, 2 * g + j], bank[6 + j][:], ACT.Copy,
                                     scale=0.5).then_inc(ga_act.sem, 1)

                for h in range(GLA_HEADS + 1):
                    g = h - 1
                    for t in range(HEAD_TILES):
                        n = HEAD_TILES * h + t
                        high(half, n + AHEAD)
                        if h < GLA_HEADS:
                            if t == 1:
                                alpha_ln(h)
                            if t < 2:
                                g_out(h, t)
                            elif t < 4:
                                v_out(h, t - 2)
                            if t == 3:
                                alpha_exp(h)
                        else:
                            act.wait_ge(tile_done.sem, tile_done.at(half * TILES + n, "t"))
                            a.activation(gate[:, t], bank[n % DBANKS][:], ACT.Tanh,
                                         scale=0.5).then_inc(evac[n % DBANKS].sem, 1)
                        if g >= 0 and t == 3:
                            gla_norm_out(g)
                        if g >= 0 and t == 5:
                            gla_high_out(g)
                for c in range(HEAD_TILES, KB):
                    n = N_GATE_A + c
                    high(half, n + AHEAD)
                    act.wait_ge(tile_done.sem, tile_done.at(half * TILES + n, "t"))
                    a.activation(gate[:, c], bank[n % DBANKS][:], ACT.Tanh,
                                 scale=0.5).then_inc(evac[n % DBANKS].sem, 1)
                for c in range(KB):
                    high(half, N_BRANCH_A + c + AHEAD)

                def qk_norm(p, t, n):
                    R = qk_round(half, p, t)
                    act.wait_ge(tile_done.sem, tile_done.at(half * TILES + n, "t"))
                    if t >= 2 or p > 0:
                        act.wait_ge(sn_dve.sem, sn_dve.at(R - 2, "n"))
                    a.activation(qk_raw[:, (5 * p + t) % 2], bank[n % DBANKS][:],
                                 ACT.Copy).then_inc(evac[n % DBANKS].sem, 1)

                def qk_square(p, t, n):
                    R = qk_round(half, p, t)
                    slot = (5 * p + t) % 2
                    act.wait_ge(evac[(n) % DBANKS].sem, left(half, n))
                    act.wait_ge(sn_pe.sem, sn_pe.at(R - 1, "s"))
                    a.activation(sq_ring[:, 0], qk_raw[:, slot], ACT.Square).then_inc(sn_act.sem, 1)

                def qk_rs(p, t):
                    R = qk_round(half, p, t)
                    act.wait_ge(sn_pe.sem, sn_pe.at(R, "s"))
                    a.activation(bank[2][:], bank[2][:], ACT.Ln, bias=eps[:], scale=1.0 / HD).then_inc(sn_act.sem, 1)
                    act.wait_ge(sn_act.sem, sn_act.at(R, "ln"))
                    a.activation(bank[2][:], bank[2][:], ACT.Exp, scale=-0.5).then_inc(sn_act.sem, 1)

                def make_bias(p, step):
                    R = swa_round(half, p)
                    width = 2 * P if step == "b" else P
                    if step == "b":
                        act.wait_ge(sm_dve.sem, sm_dve.at(unit_round(half, p, 0) - 1, "ttr"))
                    else:
                        act.wait_ge(sm_dve.sem, sm_dve.at(unit_round(half, p, 1), "ttr"))
                    for i in range(PAIR_HEADS):
                        a.activation(bias[:, i, 0:width], dist[:, 0:width], ACT.Copy,
                                     scale=slopes[PAIR_HEADS * p + i] * HD ** 0.5).then_inc(bias_act.sem, 1)

                def soft_exp(p, u):
                    R = unit_round(half, p, u)
                    b, jj = u // 2, u % 2
                    d = den[:, b % 2].rearrange("q (r j e) -> q r j e", r=2, j=2)
                    act.wait_ge(sm_dve.sem, sm_dve.at(R, "neg"))
                    if u >= 4 or p > 0:
                        act.wait_ge(dn_dve.sem, dn_dve.at(R - 4, "inv"))
                    for i in range(4):
                        r, e = i // 2, i % 2
                        a.activation(prob[:, u % 2, i], prob[:, u % 2, i], ACT.Exp, bias=m_neg[:, u % 2, i:i + 1],
                                     accum_out=d[:, r, jj, e:e + 1]).then_inc(sm_act.sem, 1)
                    act.wait_ge(sm_dve.sem, sm_dve.at(R, "gap"))
                    a.activation(s_exp[:, u % 2], s_gap[:, u % 2], ACT.Exp).then_inc(sm_act.sem, 1)

                def pt_out(p, u):
                    R = unit_round(half, p, u)
                    act.wait_ge(pt_pe.sem, pt_pe.at(R, "t", 1))
                    act.wait_ge(pv_pe.sem, pv_pe.at(R - 1, "o"))
                    a.activation(probT[:, 2:4].rearrange("q a k c -> q (a k c)"), bank[6][:],
                                 ACT.Copy).then_inc(pt_act.sem, 1)

                def swa_high_out(p, b):
                    R = block_round(half, p, b)
                    act.wait_ge(so_pe.sem, so_pe.at(R, "t"))
                    a.activation(act_o[0][:, 4 * p:4 * p + 4, b * P:(b + 1) * P], by_tt[2],
                                 ACT.Copy).then_inc(so_hi.sem, 1)

                def swa_slot(p, s):
                    if s == 2:
                        make_bias(p, "again")
                    if s < UNITS:
                        soft_exp(p, s)
                    if 1 <= s <= UNITS:
                        pt_out(p, s - 1)
                    if s % 2 == 1 and 0 <= (s - 5) // 2 < TT:
                        swa_high_out(p, (s - 5) // 2)

                a.preload_act_table_set(LN_EXP)
                for p in range(PAIRS):
                    R = swa_round(half, p)
                    for t in range(HEAD_TILES):
                        n = N_SWA + p * HEAD_TILES + t
                        high(half, n + AHEAD)
                        if t == 0 and p > 0:
                            qk_rs(p - 1, 4)
                            make_bias(p - 1, "b")
                        if t == 1 or t > 2:
                            qk_rs(p, 0 if t == 1 else t - 2)
                        if p > 0:
                            swa_slot(p - 1, 2 * t)
                        if t == 1:
                            act.wait_ge(tile_done.sem, tile_done.at(half * TILES + n, "t"))
                            act.wait_ge(sv_pe.sem, sv_pe.at(R - 1, "t"))
                            a.activation(svT[:], bank[n % DBANKS][:], ACT.Copy).then_inc(evac[n % DBANKS].sem, 1)
                        else:
                            i = 0 if t == 0 else t - 1
                            qk_norm(p, i, n)
                            qk_square(p, i, n)
                        if p > 0:
                            swa_slot(p - 1, 2 * t + 1)
                for c in range(KB):
                    n = N_GATE_B + c
                    high(half, n + AHEAD)
                    if c == 0:
                        qk_rs(PAIRS - 1, 4)
                        make_bias(PAIRS - 1, "b")
                    swa_slot(PAIRS - 1, 2 * c)
                    act.wait_ge(tile_done.sem, tile_done.at(half * TILES + n, "t"))
                    if c == 0:
                        act.wait_ge(fin_pe.sem, fin_pe.at(half - 1, "t"))
                    a.activation(resid[:, c], bank[n % DBANKS][:], ACT.Tanh,
                                 scale=0.5).then_inc(evac[n % DBANKS].sem, 1)
                    swa_slot(PAIRS - 1, 2 * c + 1)
                for c in range(KB):
                    n = N_BRANCH_B + c
                    high(half, n + AHEAD)
                    act.wait_ge(mg_dve.sem, mg_dve.at(half * KB + c, "add"))
                    a.activation(act_m[0][:, c], bank[n % DBANKS][:], ACT.Copy, scale=0.5).then_inc(mg_act.sem, 1)
                    if c % 4 == 3:
                        i = c // 4
                        act.wait_ge(mg_dve.sem, mg_dve.at(half * KB + c, "add"))
                        act.dma_start(gate[:, i * TT:(i + 1) * TT],
                                      x_rows(half)[:, :, i * T:(i + 1) * T]).then_inc(res_loaded[i], 16)

                a.preload_act_table_set(LN_EXP)

                def high_mlp(n, turn):
                    N = half * TILES + turn * TURN_TILES + n
                    occurrence = half * (TILES // RSLOTS) + turn * (TURN_TILES // RSLOTS) + n // RSLOTS
                    act.wait_ge(raw_loaded[n % RSLOTS], occurrence * 16 + 16)
                    act.wait_ge(tile_done.sem, tile_done.at(N - WSLOTS, "t"))
                    a.activation(w_hi[:, n % WSLOTS], w_raw[:, n % RSLOTS], ACT.Copy).then_inc(w_hi_done.sem, 1)

                for c in range(KB):
                    high_mlp(N_OUT + c + AHEAD, 0)
                    act.wait_ge(res_pe.sem, res_pe.at(half, "t", c))
                    a.activation(resid[:, c], bank[2 + c % 2][:], ACT.Copy).then_inc(res_copy.sem, 1)
                    act.wait_ge(evac[(N_OUT + c) % DBANKS].sem, left(half, N_OUT + c))
                    a.activation(act_x[0][:, c], resid[:, c], ACT.Copy,
                                 scale=cols[:, C_MLP + c:C_MLP + c + 1]).then_inc(hm_hi.sem, 1)
                    if c > 2:
                        act.wait_ge(hm_add.sem, hm_add.at(half, "a", c - 3))
                    a.activation(sq_sum[:] if c == 0 else sq_ring[:, c % 2], resid[:, c],
                                 ACT.Square).then_inc(hm_sq.sem, 1)

                act.wait_ge(res_pe.sem, res_pe.at(half, "t"))
                for t in range(TT):
                    act.dma_start(x_tok[:, t:t + 1],
                                  x_rows(HALVES - 1 - half)[:, t:t + 1]).then_inc(x_loaded[t], 16)

                def up_out(j, turn):
                    R = up_round(half, turn, j)
                    act.wait_ge(up_relu.sem, up_relu.at(R, "r"))
                    a.activation(bank[j % DBANKS][:], relu[:, j % 2], ACT.Square).then_inc(up_sq.sem, 1)
                    a.activation(act_o[0][:, j], relu[:, j % 2], ACT.Square).then_inc(up_sq.sem, 1)

                for j in range(KB):
                    high_mlp(N_MLP + j + AHEAD, 0)
                    if j == 0:
                        act.wait_ge(hm_sum.sem, hm_sum.at(half, "s"))
                        a.activation(rs_mlp[:], bank[6][:], ACT.Ln, bias=eps[:],
                                     scale=1.0 / D_MODEL).then_inc(hm_rs.sem, 1)
                        act.wait_ge(hm_rs.sem, hm_rs.at(half, "ln"))
                        a.activation(rs_mlp[:], rs_mlp[:], ACT.Exp, scale=-0.5).then_inc(hm_rs.sem, 1)
                    up_out(j, 0)
                    if j >= KB - TT:
                        token_square(half + 1, j - (KB - TT))
                token_rs(half + 1)
                with nc.scalar.Fori(0, MLP_TURNS - 1) as turn:
                    for c in range(KB):
                        high_mlp(N_MLP + KB + c + AHEAD, turn)
                    for j in range(KB):
                        high_mlp(N_MLP + 2 * KB + j + AHEAD, turn)
                        up_out(j, turn + 1)

                def final_copy(c):
                    act.wait_ge(fin_pe.sem, fin_pe.at(half, "t", c))
                    act.wait_ge(stored[c % 2], half * (16 * KB // 2) + 16 * (c // 2) + 16)
                    a.activation(o_stage[:, c % 2], by_tt[2 + c % 2], ACT.Copy).then_inc(fin_act.sem, 1)

                def store(c):
                    act.wait_ge(fin_act.sem, fin_act.at(half, "c", c))
                    act.dma_start(out[0].rearrange("(h t p) d -> h p t d", h=HALVES, p=P)
                                  [bass.ds(half, 1), :, :, c * P:(c + 1) * P].rearrange("h p t d -> p (h t) d"),
                                  o_stage[:, c % 2]).then_inc(stored[c % 2], 16)

                for c in range(KB):
                    if c + AHEAD < KB:
                        high_mlp(N_MLP + KB + c + AHEAD, MLP_TURNS - 1)
                    if c > 1:
                        store(c - 2)
                    x_high(half + 1, c)
                    if c > 0:
                        final_copy(c - 1)
                store(KB - 2)
                final_copy(KB - 1)
                store(KB - 1)

        @block.vector
        def _(dve):
            v = nc.vector
            for s in (evac + [xn_diag, xn_lo, hm_lo, hm_add, up_relu, shifted, al_dve, v_copy, ga_dve, ga_lo, sn_dve, sv_copy,
                              past_dve, bias_dve, sm_dve, dn_dve, pt_dve, so_dve, so_lo, mg_dve]):
                s.start(dve)
            dve.wait_ge(cols_pe, 2)
            v.tensor_copy(cols[:], bank[2][:, 0:C_ALL]).then_inc(cols_dve, 1)
            v.tensor_copy(sink[:], bank[3][:, 0:SWA_HEADS]).then_inc(cols_dve, 1)
            dve.wait_ge(const_done, 3)
            v.tensor_tensor(wa_lo[:], wa_raw[:], wa_hi[:].bitcast(F32), ALU.subtract).then_inc(cols_dve, 1)
            v.memset(dist[0:CHUNK, P + CHUNK:], NEG).then_inc(cols_dve, 1)
            v.memset(dist[CHUNK:P, 0:CHUNK], NEG).then_inc(cols_dve, 1)
            dve.wait_ge(cols_dve, 5)

            def token_scale(R, t):
                if t == 0:
                    dve.wait_ge(xn_stat.sem, xn_stat.at(R, "rs"))
                v.tensor_scalar(x_diag[:, t], ident[:], x_rs[:, t:t + 1], None, ALU.mult).then_inc(xn_diag.sem, 1)

            def x_low(R, k):
                dve.wait_ge(xn_hi.sem, xn_hi.at(R, "h", k))
                v.scalar_tensor_tensor(act_x[1][:, k], bank[4 + k % 4][:], cols[:, C_MIX + k:C_MIX + k + 1],
                                       act_x[0][:, k].bitcast(F32), ALU.mult, ALU.subtract).then_inc(xn_lo.sem, 1)

            for t in range(TT):
                token_scale(0, t)
            for k in range(KB):
                x_low(0, k)

            with nc.vector.Fori(0, HALVES) as half:
                v.tensor_copy(k_win[:, :, 0:P], k_win[:, :, T:T + P]).then_inc(shifted.sem, 1)
                v.tensor_copy(v_win[:, :, 0], v_win[:, :, TT]).then_inc(shifted.sem, 1)

                def alpha(h):
                    R = gla_round(half, h)
                    dve.wait_ge(al_act.sem, al_act.at(R, "abs"))
                    v.tensor_scalar(t_b[:], bank[2][:], cols[:, C_BA + h:C_BA + h + 1], 0.0, ALU.add,
                                    ALU.min).then_inc(al_dve.sem, 1)
                    dve.wait_ge(al_act.sem, al_act.at(R, "ln"))
                    dve.wait_ge(al_dve.sem, al_dve.at(R, "zmin"))
                    v.tensor_tensor(t_b[:], t_b[:], t_a[:], ALU.subtract).then_inc(al_dve.sem, 1)
                    dve.wait_ge(al_dve.sem, al_dve.at(R, "la"))
                    for b in range(TT):
                        v.tensor_tensor_scan(cum[:, b * P:(b + 1) * P], restart[:], t_b[:, b * P:(b + 1) * P], 0.0,
                                             ALU.mult, ALU.add).then_inc(al_dve.sem, 1)
                    dve.wait_ge(al_dve.sem, al_dve.at(R, "scan"))
                    by_chunk = cum[:].rearrange("p (c s) -> p c s", s=CHUNK)
                    total = by_chunk[:, :, CHUNK - 1:CHUNK].to_broadcast([P, NCH, CHUNK])
                    v.tensor_tensor(t_b[:].rearrange("p (c s) -> p c s", s=CHUNK), by_chunk, total,
                                    ALU.subtract).then_inc(al_dve.sem, 1)

                def v_tokens(h, j):
                    dve.wait_ge(v_pe.sem, v_pe.at(gla_round(half, h), "t", j))
                    v.tensor_copy(v_tok[:, :, j * P:(j + 1) * P], by_tt[3]).then_inc(v_copy.sem, 1)

                def silu_out(h, j):
                    n = HEAD_TILES * h + j
                    dve.wait_ge(g_tanh.sem, g_tanh.at(gla_round(half, h), "t", j))
                    v.scalar_tensor_tensor(silu[:, h % 2, j], silu[:, h % 2, j], 1.0, bank[n % DBANKS][:],
                                           ALU.add, ALU.mult).then_inc(evac[n % DBANKS].sem, 1)

                def q_out(h):
                    n = HEAD_TILES * h + 4
                    dve.wait_ge(tile_done.sem, tile_done.at(half * TILES + n, "t"))
                    dve.wait_ge(al_exp.sem, al_exp.at(gla_round(half, h), "e1"))
                    v.scalar_tensor_tensor(q_dec[:], bank[n % DBANKS][:], DK ** -0.5, t_a[:], ALU.mult,
                                           ALU.mult).then_inc(evac[n % DBANKS].sem, 1)

                def k_out(h):
                    n = HEAD_TILES * h + 5
                    dve.wait_ge(tile_done.sem, tile_done.at(half * TILES + n, "t"))
                    dve.wait_ge(al_exp.sem, al_exp.at(gla_round(half, h), "e2"))
                    v.tensor_tensor(k_dec[:], bank[n % DBANKS][:], cum[:], ALU.mult)
                    v.tensor_tensor(k_end[:], bank[n % DBANKS][:], t_b[:],
                                    ALU.mult).then_inc(evac[n % DBANKS].sem, 1)

                def states(g, first, last):
                    R = gla_round(half, g)
                    for c in range(first, last):
                        if c % 4 == 0:
                            dve.wait_ge(ga_pe.sem, ga_pe.at(R, "kv", c // 2 + 1))
                        if c == 0:
                            dve.wait_ge(ga_dve.sem, ga_dve.at(R, "first"))
                        else:
                            dve.wait_ge(ga_dve.sem, ga_dve.at(R, "st", c - 1))
                        dst = state[:, c + 1] if c + 1 < NCH else carry[:, g]
                        v.scalar_tensor_tensor(dst, state[:, c], decay[:, g % 2, c:c + 1],
                                               by_dv[6 + c % 2][:, c // 2 % 2], ALU.mult,
                                               ALU.add).then_inc(ga_dve.sem, 1)

                def gla_step(g, t):
                    R = gla_round(half, g)
                    if t == 0:
                        dve.wait_ge(ga_pe.sem, ga_pe.at(R, "ke"))
                        v.tensor_copy(ke_tok[:], by_tt[4]).then_inc(ga_dve.sem, 1)
                        dve.wait_ge(ga_dve.sem, ga_dve.at(R - GLA_HEADS, "st"))
                        dve.wait_ge(ga_pe.sem, ga_pe.at(R, "sc"))
                        v.tensor_copy(state[:, 0], carry[:, g]).then_inc(ga_dve.sem, 1)
                        for b in range(TT):
                            v.copy_predicated(masked[:, b], causal[:], by_tt[5][:, b]).then_inc(ga_dve.sem, 1)
                    if t == 1:
                        states(g, 0, 4)
                    if t == 2:
                        states(g, 4, NCH)
                    if t == 5:
                        for j in range(2):
                            dve.wait_ge(ga_pe.sem, ga_pe.at(R, "ot", j))
                            v.scalar_tensor_tensor(bank[6 + j][:], bank[6 + j][:], cols[:, C_GN + j:C_GN + j + 1],
                                                   silu[:, g % 2, j], ALU.mult, ALU.mult).then_inc(ga_dve.sem, 1)
                    if t == 6:
                        for j in range(2):
                            dve.wait_ge(ga_act.sem, ga_act.at(R, "hi", j))
                            v.scalar_tensor_tensor(act_o[1][:, 2 * g + j], bank[6 + j][:], 0.5,
                                                   act_o[0][:, 2 * g + j].bitcast(F32), ALU.mult,
                                                   ALU.subtract).then_inc(ga_lo.sem, 1)

                for h in range(GLA_HEADS + 1):
                    for t in range(HEAD_TILES):
                        if h > 0:
                            if t == 5 and h < GLA_HEADS:
                                dve.wait_ge(evac[(HEAD_TILES * h + 1) % DBANKS].sem, left(half, HEAD_TILES * h + 1))
                            elif t == 5:
                                dve.wait_ge(evac[(HEAD_TILES * (h - 1) + 5) % DBANKS].sem, left(half, HEAD_TILES * (h - 1) + 5))
                            gla_step(h - 1, t)
                        if h < GLA_HEADS:
                            if t < 2:
                                silu_out(h, t)
                            if t == 2:
                                alpha(h)
                            if t == 3 or t == 4:
                                v_tokens(h, t - 3)
                            if t == 4:
                                q_out(h)
                            if t == 5:
                                k_out(h)
                        if h > 0 and t == 5:
                            gla_step(h - 1, 6)
                for c in range(KB):
                    n = N_BRANCH_A + c
                    dve.wait_ge(tile_done.sem, tile_done.at(half * TILES + n, "t"))
                    v.scalar_tensor_tensor(gate[:, c], gate[:, c], 1.0, bank[n % DBANKS][:], ALU.add,
                                           ALU.mult).then_inc(evac[n % DBANKS].sem, 1)

                def qk_out(p, i):
                    R = qk_round(half, p, i)
                    dve.wait_ge(sn_act.sem, sn_act.at(R, "rs"))
                    if p > 0 and i > 0:
                        dve.wait_ge(sc_pe.sem, sc_pe.at(unit_round(half, p - 1, UNITS - 2 + (i - 1) // 2), "s"))
                    dst = k_win[:, p, P:] if i == 0 else qT[:, i - 1]
                    gain = C_KN if i == 0 else C_QN
                    v.scalar_tensor_tensor(dst, qk_raw[:, (5 * p + i) % 2], cols[:, gain:gain + 1], bank[2][:],
                                           ALU.mult, ALU.mult).then_inc(sn_dve.sem, 1)

                def swa_slot(p, s):
                    if s == 0:
                        dve.wait_ge(bias_act.sem, bias_act.at(swa_round(half, p), "b"))
                        dve.wait_ge(past_dve.sem, past_dve.at(half - 1, "off"))
                        v.tensor_scalar(bias[:, :, 0:P], bias[:, :, 0:P], no_past[:], None,
                                        ALU.add).then_inc(bias_dve.sem, 1)
                        dve.wait_ge(bias_dve.sem, bias_dve.at(swa_round(half, p), "past"))
                    if s < UNITS:
                        b, jj = s // 2, s % 2
                        R = unit_round(half, p, s)
                        dve.wait_ge(sc_pe.sem, sc_pe.at(R, "s"))
                        dve.wait_ge(pt_pe.sem, pt_pe.at(R - 2, "t"))
                        if s == 2:
                            dve.wait_ge(bias_act.sem, bias_act.at(swa_round(half, p), "again"))
                        sinks = sink[:].rearrange("q (p r j e) -> q p r j e", p=PAIRS, r=2, j=2)[:, p, :, jj]
                        two = lambda a: a[:, s % 2].rearrange("q (r e) -> q r e", r=2)
                        v.tensor_copy(two(s_sink), sinks).then_inc(sm_dve.sem, 1)
                        for i in range(4):
                            r, e = i // 2, i % 2
                            v.tensor_tensor_reduce(prob[:, s % 2, i], bank[3 + r][:, e * 2 * P:(e + 1) * 2 * P],
                                                   bias[:, 4 * r + 2 * jj + e], HD ** -0.5, -3.0e38, ALU.add,
                                                   ALU.max, mx[:, s % 2, i:i + 1]).then_inc(sm_dve.sem, 1)
                        dve.wait_ge(sm_dve.sem, sm_dve.at(R, "ttr"))
                        v.tensor_tensor(m_all[:, s % 2], mx[:, s % 2], s_sink[:, s % 2], ALU.max).then_inc(sm_dve.sem, 1)
                        dve.wait_ge(sm_dve.sem, sm_dve.at(R, "m"))
                        v.tensor_scalar(m_neg[:, s % 2], m_all[:, s % 2], -1.0, None,
                                        ALU.mult).then_inc(sm_dve.sem, 1)
                        v.tensor_tensor(s_gap[:, s % 2], s_sink[:, s % 2], m_all[:, s % 2], ALU.subtract).then_inc(sm_dve.sem, 1)
                    if 1 <= s <= UNITS:
                        u = s - 1
                        b, jj = u // 2, u % 2
                        R = unit_round(half, p, u)
                        dve.wait_ge(sm_act.sem, sm_act.at(R, "sink"))
                        sub = lambda a: a[:, b % 2].rearrange("q (r j e) -> q r j e", r=2, j=2)[:, :, jj]
                        all_ = den_all[:, u % 2].rearrange("q (r e) -> q r e", r=2)
                        v.tensor_tensor(all_, sub(den), s_exp[:, u % 2].rearrange("q (r e) -> q r e", r=2),
                                        ALU.add).then_inc(dn_dve.sem, 1)
                        dve.wait_ge(dn_dve.sem, dn_dve.at(R, "sum"))
                        v.reciprocal(sub(den_inv), all_).then_inc(dn_dve.sem, 1)
                        dve.wait_ge(pt_pe.sem, pt_pe.at(R, "t", 0))
                        dve.wait_ge(pv_pe.sem, pv_pe.at(R - 1, "o"))
                        v.tensor_copy(probT[:, 0:2].rearrange("q a k c -> q (a k c)"),
                                      bank[5][:]).then_inc(pt_dve.sem, 1)
                    if s % 2 == 1 and 0 <= (s - 3) // 2 < TT:
                        b = (s - 3) // 2
                        dve.wait_ge(pv_pe.sem, pv_pe.at(unit_round(half, p, 2 * b + 1), "o"))
                        dve.wait_ge(dn_dve.sem, dn_dve.at(unit_round(half, p, 2 * b + 1), "inv"))
                        v.tensor_tensor(s_tok[:, b % 2], bank[7][:].rearrange("q (h d) -> q h d", d=HD),
                                        den_inv[:, b % 2].rearrange("q (h o) -> q h o", o=1)
                                        .to_broadcast([P, 8, HD]), ALU.mult).then_inc(so_dve.sem, 1)
                    if s % 2 == 1 and 0 <= (s - 5) // 2 < TT:
                        b = (s - 5) // 2
                        dve.wait_ge(so_hi.sem, so_hi.at(block_round(half, p, b), "h"))
                        at = (slice(None), slice(4 * p, 4 * p + 4), slice(b * P, (b + 1) * P))
                        v.tensor_tensor(act_o[1][at], by_tt[2], act_o[0][at].bitcast(F32),
                                        ALU.subtract).then_inc(so_lo.sem, 1)

                for p in range(PAIRS):
                    for t in range(HEAD_TILES):
                        if t == 0 and p > 0:
                            qk_out(p - 1, 4)
                        if t == 1 or t > 2:
                            qk_out(p, 0 if t == 1 else t - 2)
                        if t == 2:
                            R = swa_round(half, p)
                            dve.wait_ge(sv_pe.sem, sv_pe.at(R, "t"))
                            v.tensor_copy(v_win[:, p, 1:], by_tt[2]).then_inc(sv_copy.sem, 1)
                        if p > 0:
                            swa_slot(p - 1, 2 * t)
                            swa_slot(p - 1, 2 * t + 1)
                qk_out(PAIRS - 1, 4)
                for s in range(12):
                    swa_slot(PAIRS - 1, s)
                v.memset(no_past[:], 0.0).then_inc(past_dve.sem, 1)

                for c in range(KB):
                    n = N_BRANCH_B + c
                    b = bank[n % DBANKS][:]
                    R = half * KB + c
                    dve.wait_ge(tile_done.sem, tile_done.at(half * TILES + n, "t"))
                    v.scalar_tensor_tensor(b, resid[:, c], 1.0, b, ALU.add, ALU.mult).then_inc(mg_dve.sem, 1)
                    dve.wait_ge(mg_dve.sem, mg_dve.at(R, "mul"))
                    v.tensor_tensor(b, b, gate[:, c], ALU.add).then_inc(mg_dve.sem, 1)
                    dve.wait_ge(mg_act.sem, mg_act.at(R, "hi"))
                    v.scalar_tensor_tensor(act_m[1][:, c], b, 0.5, act_m[0][:, c].bitcast(F32), ALU.mult,
                                           ALU.subtract).then_inc(evac[n % DBANKS].sem, 1)
                for c in range(KB):
                    n = N_OUT + c
                    dve.wait_ge(res_copy.sem, res_copy.at(half, "c", c))
                    dve.wait_ge(tile_done.sem, tile_done.at(half * TILES + n, "t"))
                    v.tensor_tensor(resid[:, c], bank[n % DBANKS][:], resid[:, c],
                                    ALU.add).then_inc(evac[n % DBANKS].sem, 1)
                    dve.wait_ge(hm_hi.sem, hm_hi.at(half, "h", c))
                    v.scalar_tensor_tensor(act_x[1][:, c], resid[:, c], cols[:, C_MLP + c:C_MLP + c + 1],
                                           act_x[0][:, c].bitcast(F32), ALU.mult,
                                           ALU.subtract).then_inc(hm_lo.sem, 1)
                    if c > 0:
                        dve.wait_ge(hm_sq.sem, hm_sq.at(half, "s", c))
                        if c > 1:
                            dve.wait_ge(hm_add.sem, hm_add.at(half, "a", c - 2))
                        v.tensor_tensor(sq_sum[:], sq_sum[:], sq_ring[:, c % 2], ALU.add).then_inc(hm_add.sem, 1)

                def up_out(j, n, turn, up_turn):
                    R = up_round(half, up_turn, j)
                    dve.wait_ge(tile_done.sem, tile_done.at(half * TILES + turn * TURN_TILES + n, "t"))
                    v.scalar_tensor_tensor(relu[:, j % 2], bank[n % DBANKS][:], 0.0, rs_mlp[:], ALU.max,
                                           ALU.mult).then_inc(up_relu.sem, 1)
                    dve.wait_ge(up_sq.sem, up_sq.at(R, "hi"))
                    v.tensor_tensor(act_o[1][:, j], bank[n % DBANKS][:], act_o[0][:, j].bitcast(F32),
                                    ALU.subtract).then_inc(evac[n % DBANKS].sem, 1)

                def down_out(c, turn):
                    n = N_MLP + KB + c
                    dve.wait_ge(tile_done.sem, tile_done.at(half * TILES + turn * TURN_TILES + n, "t"))
                    dve.wait_ge(evac[(n - 1) % DBANKS].sem, left(half, n - 1, turn))
                    v.tensor_tensor(resid[:, c], bank[n % DBANKS][:], resid[:, c],
                                    ALU.add).then_inc(evac[n % DBANKS].sem, 1)

                dve.wait_ge(hm_rs.sem, hm_rs.at(half, "rs"))
                for j in range(KB):
                    up_out(j, N_MLP + j, 0, 0)
                for t in range(TT):
                    token_scale(half + 1, t)
                with nc.vector.Fori(0, MLP_TURNS - 1) as turn:
                    for c in range(KB):
                        down_out(c, turn)
                    for j in range(KB):
                        up_out(j, N_MLP + 2 * KB + j, turn, turn + 1)
                for c in range(KB):
                    x_low(half + 1, c)
                    down_out(c, MLP_TURNS - 1)

        @block.tensor
        def _(pe):
            t_ = nc.tensor
            for s in (tile_done, xn_pe, res_pe, hm_sum, lr_pe, al_pe, v_pe, ga_pe, sn_pe, sv_pe, sc_pe, pt_pe, pv_pe, so_pe,
                      fin_pe):
                s.start(pe)
            pe.wait_ge(const_pool, POOL_CONSTS)
            pe.wait_ge(const_dma, CONST_DMAS * 16)
            t_.transpose(bank[2][:, 0:C_ALL], rows[:], ident[0:C_ALL, 0:C_ALL]).then_inc(cols_pe, 1)
            t_.matmul(bank[3][:, 0:SWA_HEADS], ones[0:1, :], sink_row[:], start=True,
                      stop=True).then_inc(cols_pe, 1)
            pe.wait_ge(cols_dve, 5)

            def dense(half, n, src, mid=None, turn=0, ready=None):
                N = half * TILES + turn * TURN_TILES + n
                pe.wait_ge(w_lo_done.sem, w_lo_done.at(N, "w"))
                pe.wait_ge(evac[n % DBANKS].sem, left(half, n - DBANKS, turn))
                hi, lo = w_hi[:, n % WSLOTS], w_lo[:, n % WSLOTS]
                o = bank[n % DBANKS][:]
                for k in range(KB):
                    if k == KB // 2 and mid:
                        mid()
                    if ready:
                        ready(k)
                    t_.matmul(o, hi[:, k], src[0][:, k], start=k == 0, stop=False)
                    t_.matmul(o, lo[:, k], src[0][:, k], start=False, stop=False)
                    last = t_.matmul(o, hi[:, k], src[1][:, k], start=False, stop=k == KB - 1)
                last.then_inc(tile_done.sem, 1)

            def transposes(dst, src_of, n=TT):
                for b in range(n):
                    last = t_.transpose(dst[:, b], src_of(b), ident[:])
                return last

            def x_scaled(R, k):
                if k == 0:
                    pe.wait_ge(xn_diag.sem, xn_diag.at(R, "d"))
                if k >= 4:
                    pe.wait_ge(xn_lo.sem, xn_lo.at(R, "l", k - 4))
                for b in range(TT):
                    last = t_.matmul(by_tt[4 + k % 4][:, b], x_tok[:, b, k * P:(k + 1) * P], x_diag[:, b],
                                     start=True, stop=True)
                last.then_inc(xn_pe.sem, 1)

            for k in range(KB):
                x_scaled(0, k)

            with nc.tensor.Fori(0, HALVES) as half:
                pe.wait_ge(fin_act.sem, fin_act.at(half - 1, "c", KB - 2))
                for k in range(KB):
                    cut = slice(k * RANK, k * RANK + P)
                    pe.wait_ge(xn_lo.sem, xn_lo.at(half, "l", k))
                    t_.matmul(bank[2][:], wa_hi[:, cut], act_x[0][:, k], start=k == 0, stop=False)
                    t_.matmul(bank[2][:], wa_lo[:, cut], act_x[0][:, k], start=False, stop=False)
                    last = t_.matmul(bank[2][:], wa_hi[:, cut], act_x[1][:, k], start=False, stop=k == KB - 1)
                last.then_inc(lr_pe.sem, 1)

                def alpha(h):
                    R = gla_round(half, h)
                    if h == 0:
                        pe.wait_ge(lr_copy.sem, lr_copy.at(half, "t"))
                    else:
                        pe.wait_ge(al_dve.sem, al_dve.at(R - 1, "zmin"))
                    t_.matmul(bank[2][:], w_a2[:, h * DK:(h + 1) * DK], a_low[:], start=True,
                              stop=True).then_inc(al_pe.sem, 1)

                def v_turn(h, j):
                    R = gla_round(half, h)
                    pe.wait_ge(evac[(HEAD_TILES * h + 2 + j) % DBANKS].sem, left(half, HEAD_TILES * h + 2 + j))
                    if h == 0 and j == 0:
                        pe.wait_ge(fin_act.sem, fin_act.at(half - 1, "c"))
                    if j == 0:
                        pe.wait_ge(v_copy.sem, v_copy.at(R - 1, "t", 1))
                    else:
                        pe.wait_ge(v_copy.sem, v_copy.at(R, "t", 0))
                    transposes(by_tt[3], lambda b: vT[:, b * P:(b + 1) * P]).then_inc(v_pe.sem, 1)

                def gla_slot(g, s):
                    R = gla_round(half, g)
                    vt = v_tok
                    if s == 0:
                        pe.wait_ge(evac[(HEAD_TILES * g + 5) % DBANKS].sem, left(half, HEAD_TILES * g + 5))
                        pe.wait_ge(ga_act.sem, ga_act.at(R - 1, "o"))
                        transposes(by_tt[4], lambda b: k_end[:, b * P:(b + 1) * P]).then_inc(ga_pe.sem, 1)
                        for b in range(TT):
                            c = slice(b * P, (b + 1) * P)
                            last = t_.matmul(by_tt[5][:, b], k_dec[:, c], q_dec[:, c], start=True, stop=True)
                        last.then_inc(ga_pe.sem, 1)
                    if s == 1 or s == 3:
                        if s == 1:
                            pe.wait_ge(ga_dve.sem, ga_dve.at(R, "ke"))
                            pe.wait_ge(v_copy.sem, v_copy.at(R, "t", 1))
                            pe.wait_ge(ga_lo.sem, ga_lo.at(R - 1, "lo"))
                        else:
                            pe.wait_ge(ga_dve.sem, ga_dve.at(R, "st", 3))
                        for i in ((0, 1) if s == 1 else (2, 3)):
                            for c in (2 * i, 2 * i + 1):
                                r = slice(c % 2 * CHUNK, c % 2 * CHUNK + CHUNK)
                                last = t_.matmul(by_dv[6 + c % 2][:, i % 2], ke_tok[r, i], vt[r, i], start=True,
                                                 stop=True)
                            last.then_inc(ga_pe.sem, 1)
                    if s == 5 or s == 6:
                        pe.wait_ge(ga_dve.sem, ga_dve.at(R, "mask"))
                        pe.wait_ge(ga_dve.sem, ga_dve.at(R, "st", NCH - 2))
                        for b in ((0, 1) if s == 5 else (2, 3)):
                            o = by_dv[4 + b // 2][:, b % 2]
                            t_.matmul(o, masked[:, b], vt[:, b], start=True, stop=False, skip_group_check=True)
                            for c in (2 * b, 2 * b + 1):
                                r = slice(c % 2 * CHUNK, c % 2 * CHUNK + CHUNK)
                                last = t_.matmul(o[r], q_dec[:, c * CHUNK:(c + 1) * CHUNK], state[:, c],
                                                 start=False, stop=True, skip_group_check=True)
                        last.then_inc(ga_pe.sem, 1)
                    if s == 10:
                        pe.wait_ge(ga_act.sem, ga_act.at(R, "o"))
                        pe.wait_ge(ga_dve.sem, ga_dve.at(R, "st"))
                        for j in range(2):
                            transposes(by_tt[6 + j],
                                       lambda b: o_tok[:, b, j * P:(j + 1) * P]).then_inc(ga_pe.sem, 1)

                for h in range(GLA_HEADS + 1):
                    for t in range(HEAD_TILES):
                        def slot(s):
                            if h > 0:
                                gla_slot(h - 1, s)
                            if h < GLA_HEADS and s == 2:
                                alpha(h)
                            if h < GLA_HEADS and s in (6, 8):
                                v_turn(h, (s - 6) // 2)
                        dense(half, HEAD_TILES * h + t, act_x, lambda: slot(2 * t))
                        slot(2 * t + 1)
                for c in range(HEAD_TILES, KB):
                    dense(half, N_GATE_A + c, act_x)
                pe.wait_ge(ga_lo.sem, ga_lo.at(gla_round(half, GLA_HEADS - 1), "lo"))
                for c in range(KB):
                    dense(half, N_BRANCH_A + c, act_o)

                def qk_sum(p, i):
                    R = qk_round(half, p, i)
                    pe.wait_ge(sn_act.sem, sn_act.at(R, "sq"))
                    if i == 0 and p > 0:
                        pe.wait_ge(sn_dve.sem, sn_dve.at(R - 1, "n"))
                    if i == 1 and p == 0:
                        pe.wait_ge(sv_copy.sem, sv_copy.at(swa_round(half, p), "t"))
                    if i > 1 and p == 0:
                        pe.wait_ge(sn_dve.sem, sn_dve.at(R - 1, "n"))
                    if i > 0 and p > 0:
                        pe.wait_ge(so_lo.sem, so_lo.at(block_round(half, p - 1, i - 1), "l"))
                    t_.matmul(bank[2][:], ones_hd[:], sq_ring[:, 0], start=True, stop=True).then_inc(sn_pe.sem, 1)

                def swa_slot(p, s):
                    if s < UNITS:
                        b, jj = s // 2, s % 2
                        R = unit_round(half, p, s)
                        pe.wait_ge(sn_dve.sem, sn_dve.at(qk_round(half, p, 2 + 2 * jj), "n"))
                        pe.wait_ge(sm_dve.sem, sm_dve.at(R - 1, "ttr"))
                        for e in range(2):
                            for r in range(2):
                                rows_ = slice(r * HD, r * HD + HD)
                                last = t_.matmul(bank[3 + r][:, e * 2 * P:(e + 1) * 2 * P],
                                                 qT[rows_, 2 * jj + e, b * P:(b + 1) * P],
                                                 k_win[rows_, p, b * P:(b + 2) * P], start=True, stop=True)
                        last.then_inc(sc_pe.sem, 1)
                    if 1 <= s <= UNITS:
                        R = unit_round(half, p, s - 1)
                        pe.wait_ge(sm_act.sem, sm_act.at(R, "p"))
                        for half_ in range(2):
                            pe.wait_ge((pt_dve, pt_act)[half_].sem, (pt_dve, pt_act)[half_].at(R - 1, "c"))
                            for i in range(2):
                                for k in range(2):
                                    last = t_.transpose(by_tt[5 + half_][:, 2 * i + k],
                                                        prob[:, (s - 1) % 2, 2 * half_ + i, k * P:(k + 1) * P],
                                                        ident[:])
                            last.then_inc(pt_pe.sem, 1)
                    if 2 <= s <= UNITS + 1:
                        u = s - 2
                        b, jj = u // 2, u % 2
                        R = unit_round(half, p, u)
                        pe.wait_ge(pt_dve.sem, pt_dve.at(R, "c"))
                        pe.wait_ge(pt_act.sem, pt_act.at(R, "c"))
                        if jj == 0:
                            pe.wait_ge(so_dve.sem, so_dve.at(block_round(half, p, b) - 1, "o"))
                            if u == 0:
                                pe.wait_ge(sv_copy.sem, sv_copy.at(swa_round(half, p), "t"))
                        for i in range(4):
                            r, e = i // 2, i % 2
                            hq = 4 * r + 2 * jj + e
                            for k in range(2):
                                last = t_.matmul(bank[7][:, hq * HD:(hq + 1) * HD], probT[:, i, k],
                                                 v_win[:, p, b + k, r * HD:(r + 1) * HD], start=k == 0, stop=k == 1)
                        last.then_inc(pv_pe.sem, 1)
                    if s % 2 == 1 and 0 <= (s - 5) // 2 < TT:
                        b = (s - 5) // 2
                        R = block_round(half, p, b)
                        pe.wait_ge(so_dve.sem, so_dve.at(R, "o"))
                        if p < PAIRS - 1 and b == 0:
                            pe.wait_ge(sv_copy.sem, sv_copy.at(swa_round(half, p + 1), "t"))
                        elif p < PAIRS - 1 or b == 0:
                            pe.wait_ge(sn_dve.sem, sn_dve.at(
                                qk_round(half, p + 1, b) if p < PAIRS - 1 else qk_round(half, p, 4), "n"))
                        else:
                            pe.wait_ge(so_lo.sem, so_lo.at(R - 1, "l"))
                        two = s_tok[:, b % 2].rearrange("q (c a) d -> q c (a d)", a=2)
                        transposes(by_tt[2], lambda c: two[:, c], 4).then_inc(so_pe.sem, 1)

                for p in range(PAIRS):
                    for t in range(HEAD_TILES):
                        def middle():
                            if t == 0 and p > 0:
                                qk_sum(p - 1, 4)
                            if t == 1 or t > 2:
                                qk_sum(p, 0 if t == 1 else t - 2)
                            if t == 2:
                                pe.wait_ge(evac[(N_SWA + p * HEAD_TILES + 1) % DBANKS].sem, left(half, N_SWA + p * HEAD_TILES + 1))
                                pe.wait_ge(sn_dve.sem, sn_dve.at(qk_round(half, p, 0), "n"))
                                transposes(by_tt[2], lambda b: svT[:, b * P:(b + 1) * P]).then_inc(sv_pe.sem, 1)
                            if p > 0:
                                swa_slot(p - 1, 2 * t)
                        dense(half, N_SWA + p * HEAD_TILES + t, act_x, middle)
                        if p > 0:
                            swa_slot(p - 1, 2 * t + 1)
                for c in range(KB):
                    def middle():
                        if c == 0:
                            qk_sum(PAIRS - 1, 4)
                        swa_slot(PAIRS - 1, 2 * c)
                    dense(half, N_GATE_B + c, act_x, middle)
                    swa_slot(PAIRS - 1, 2 * c + 1)
                pe.wait_ge(so_lo.sem, so_lo.at(block_round(half, PAIRS - 1, TT - 1), "l"))
                for c in range(KB):
                    dense(half, N_BRANCH_B + c, act_o)
                pe.wait_ge(evac[(N_BRANCH_B + KB - 1) % DBANKS].sem, left(half, N_BRANCH_B + KB - 1))
                for c in range(KB):
                    def residual():
                        if c % 4 == 0:
                            pe.wait_ge(res_loaded[c // 4], half * 16 + 16)
                        if c >= 2:
                            pe.wait_ge(res_copy.sem, res_copy.at(half, "c", c - 2))
                        transposes(by_tt[2 + c % 2], lambda b: gate[:, c // 4 * TT + b, c % 4 * P:(c % 4 + 1) * P]
                                   ).then_inc(res_pe.sem, 1)
                    dense(half, N_OUT + c, act_m, residual)

                def up(j, n, turn):
                    if n < N_MLP + KB and j == 0:
                        dense(half, n, act_x, turn=turn,
                              ready=lambda k: pe.wait_ge(hm_lo.sem, hm_lo.at(half, "l", k)))
                    else:
                        dense(half, n, act_x, turn=turn)

                def down(c, turn, mid=None):
                    def ready(k):
                        pe.wait_ge(evac[k % DBANKS].sem, left(half, N_MLP + k, turn))
                    dense(half, N_MLP + KB + c, act_o, mid, turn, ready if c == 0 else None)

                for j in range(KB):
                    up(j, N_MLP + j, 0)
                    if j == 0:
                        pe.wait_ge(hm_add.sem, hm_add.at(half, "a"))
                        t_.matmul(bank[6][:], ones[:], sq_sum[:], start=True, stop=True).then_inc(hm_sum.sem, 1)
                with nc.tensor.Fori(0, MLP_TURNS - 1) as turn:
                    for c in range(KB):
                        down(c, turn)
                    for j in range(KB):
                        up(j, N_MLP + 2 * KB + j, turn)

                def final(c):
                    n = N_MLP + KB + c
                    pe.wait_ge(evac[n % DBANKS].sem, left(half, n, MLP_TURNS - 1))
                    if c >= 2:
                        pe.wait_ge(fin_act.sem, fin_act.at(half, "c", c - 2))
                    transposes(by_tt[2 + c % 2], lambda b: resid[:, c, b * P:(b + 1) * P]).then_inc(fin_pe.sem, 1)

                for c in range(KB):
                    down(c, MLP_TURNS - 1, lambda: x_scaled(half + 1, c))
                    if c > 0:
                        final(c - 1)
                final(KB - 1)


def kernel(**inputs):
    import numpy as _np
    import concourse.bacc as _bacc
    from concourse import mybir as _mybir
    from concourse.bass_utils import run_bass_kernel_spmd as _run

    names = ["x", "norm_mix", "w_in", "w_alpha2", "b_alpha", "gla_norm", "swa_q_norm", "swa_k_norm", "swa_sinks",
             "w_branch_gla", "w_branch_swa", "w_out", "norm_mlp", "w_up", "w_down"]
    nc = _bacc.Bacc("TRN2", target_bir_lowering=False, num_devices=1)
    arrays, args = {}, []
    for name in names:
        a = _np.ascontiguousarray(inputs[name])
        arrays[f"in_{name}_dram"] = a
        args.append(nc.dram_tensor(f"in_{name}_dram", a.shape, _mybir.dt.from_np(a.dtype), kind="ExternalInput").ap())
    args.append(nc.dram_tensor("out_0_dram", (1, SEQ, D_MODEL), _mybir.dt.float32, kind="ExternalOutput").ap())
    program(nc, *args)
    r = _run(nc, [arrays], core_ids=[0])
    return r.results[0]["out_0_dram"]
```

```python
from contextlib import ExitStack

import concourse.bass as bass
from concourse import mybir

F32 = mybir.dt.float32
F32R = mybir.dt.float32r
I32 = mybir.dt.int32
ALU = mybir.AluOpType
ACT = mybir.ActivationFunctionType
AX_X = mybir.AxisListType.X

P = 128
EPS = 1e-6
NEG = -1e30
D_MODEL = 1024
SEQ = 1024
HALVES = 2
POOL_CONSTS = 18
POOL_FIRST = 3
CONST_DMAS = 12
T = SEQ // HALVES
TT = T // P
KB = D_MODEL // P
CHUNK = 64
NCH = T // CHUNK
GLA_HEADS, DK, DV, RANK = 4, 128, 256, 16
GLA_TAU = 16.0
SWA_HEADS, KV_HEADS, HD = 16, 4, 64
PAIRS = KV_HEADS // 2
PAIR_HEADS = SWA_HEADS // PAIRS
UNITS = TT * 2
D_FF = 4 * D_MODEL

GQ = 0
GK = GQ + GLA_HEADS * DK
GV = GK + GLA_HEADS * DK
GG = GV + GLA_HEADS * DV
GA = GG + GLA_HEADS * DV
SQ = GA + RANK
SK = SQ + SWA_HEADS * HD
SV = SK + KV_HEADS * HD
GATE_A = SV + KV_HEADS * HD
GATE_B = GATE_A + D_MODEL

HEAD_TILES = 6
N_GLA = 0
N_GATE_A = N_GLA + GLA_HEADS * HEAD_TILES
N_BRANCH_A = N_GATE_A + KB
N_SWA = N_BRANCH_A + KB
N_GATE_B = N_SWA + PAIRS * HEAD_TILES
N_BRANCH_B = N_GATE_B + KB
N_OUT = N_BRANCH_B + KB
N_MLP = N_OUT + KB
QUERY_TILES = [N_SWA + p * HEAD_TILES + t for p in range(PAIRS) for t in range(2, HEAD_TILES)]
MLP_TURNS = 4
TURN_TILES = 2 * KB
TILES = N_MLP + MLP_TURNS * TURN_TILES
WA_COLS = (KB - 1) * 2 * RANK + P
WSLOTS = 4
RSLOTS = 2
AHEAD = 3
DBANKS = 2

LN_EXP = "natural_log_exp_and_others"
EXP_TANH = "exp_and_others"
C_MIX, C_MLP, C_BA, C_GN, C_QN, C_KN, C_ALL = 0, 8, 16, 20, 22, 23, 24


class Stream:

    def __init__(self, sem, credit=1, **steps):
        self.sem, self.credit, self.ends, self.sizes, n = sem, credit, {}, steps, 0
        for name, size in steps.items():
            self.ends[name] = n
            n += size
        self.size = n

    def at(self, turn, step, nth=None):
        last = self.sizes[step] if nth is None else nth + 1
        return turn * self.size + (self.credit * self.size + self.ends[step] + last)

    def start(self, eng):
        eng.sem_inc(self.sem, self.credit * self.size)


def program(nc, x, norm_mix, w_in, w_alpha2, b_alpha, gla_norm, swa_q_norm, swa_k_norm, swa_sinks,
            w_branch_gla, w_branch_swa, w_out, norm_mlp, w_up, w_down, out):
    with ExitStack() as ctx:
        def sb(name, shape, dt=F32, stack=ctx):
            return stack.enter_context(nc.sbuf_tensor(name, shape, dt))

        def sem(name):
            return ctx.enter_context(nc.semaphore(name))

        def stream(name, credit=1, **steps):
            return Stream(sem(name), credit, **steps)

        resid = sb("resid", [P, KB, T])
        gate = sb("gate", [P, KB, T])
        x_tok = gate[:].rearrange("p (t a) c -> p t (a c)", t=TT)
        act_x = [sb("act_x_hi", [P, KB, T], F32R), sb("act_x_lo", [P, KB, T], F32R)]
        act_o = [sb("act_o_hi", [P, KB, T], F32R), sb("act_o_lo", [P, KB, T], F32R)]
        w_raw = sb("w_raw", [P, RSLOTS, KB, P])
        w_hi = sb("w_hi", [P, WSLOTS, KB, P], F32R)
        w_lo = sb("w_lo", [P, WSLOTS, KB, P], F32R)

        ident = sb("ident", [P, P])
        ones = sb("ones", [P, P])
        ones_hd = sb("ones_hd", [P, P])
        causal = sb("causal", [P, P], I32)
        restart = sb("restart", [P, P])
        dist = sb("dist", [P, 2 * P])
        eps = sb("eps", [P, 1])
        cols = sb("cols", [P, C_ALL])
        sink_row = sb("sink_row", [1, SWA_HEADS])
        sink = sb("sink", [P, SWA_HEADS])
        sink_neg = sb("sink_neg", [P, SWA_HEADS])
        w_a2 = sb("w_a2", [2 * RANK, GLA_HEADS * DK])
        wa_both = sb("wa_both", [P, WA_COLS], F32R)
        wa_cols = wa_both[:, 0:KB * 2 * RANK].rearrange("p (k s r) -> p k s r", k=KB, s=2)
        no_past = sb("no_past", [P, 1])
        carry = sb("carry", [P, GLA_HEADS, DV])
        masked = sb("masked", [P, TT, P])
        k_past = sb("k_past", [P, PAIRS, P])
        v_past = sb("v_past", [P, PAIRS, P])
        sq_ring = sb("sq_ring", [P, 2, T])
        svT = sq_ring[:, 1]
        o_stage = sq_ring[:].rearrange("p s (t c) -> p s t c", t=TT)

        with ExitStack() as region:
            causal_f = sb("causal_f", [P, P], F32, region)
            rows = sb("rows", [C_ALL, P], F32, region)
            wa_raw = sb("wa_raw", [P, KB, RANK], F32, region)
        with ExitStack() as region:
            vT = sb("vT", [P, T], F32, region)
            v_tok = sb("v_tok", [P, TT, DV], F32, region)
            silu = sb("silu", [P, 2, 2, T], F32, region)
            t_a = sb("t_a", [P, T], F32, region)
            t_b = sb("t_b", [P, T], F32, region)
            cum = sb("cum", [P, T], F32, region)
            decay = sb("decay", [P, 2, NCH], F32, region)
            q_dec = sb("q_dec", [P, T], F32, region)
            k_dec = sb("k_dec", [P, T], F32, region)
            k_end = sb("k_end", [P, T], F32, region)
            ke_tok = sb("ke_tok", [P, TT, P], F32, region)
            state = sb("state", [P, NCH, DV], F32, region)
            o_tok = sb("o_tok", [P, TT, DV], F32, region)
            o_ss = sb("o_ss", [P, TT], F32, region)
            o_rs = sb("o_rs", [P, TT], F32, region)
            a_low = sb("a_low", [2 * RANK, T], F32, region)
        with ExitStack() as region:
            k_win = [sb("k_win_hi", [P, PAIRS, P + T], F32R, region),
                     sb("k_win_lo", [P, PAIRS, P + T], F32R, region)]
            qk_raw = sb("qk_raw", [P, 2, T], F32, region)
            v_win = [sb("v_win_hi", [P, PAIRS, 1 + TT, P], F32R, region),
                     sb("v_win_lo", [P, PAIRS, 1 + TT, P], F32R, region)]
            bias = sb("bias", [P, PAIR_HEADS, 2 * P], F32, region)
            prob = sb("prob", [P, 2, 4, 2 * P], F32, region)
            probT = [sb("probT_hi", [P, 2, 2, 2 * P], F32R, region), sb("probT_lo", [P, 2, 2, 2 * P], F32R, region)]
            mx = sb("mx", [P, 2, 4], F32, region)
            m_neg = sb("m_neg", [P, 2, 4], F32, region)
            s_gap = sb("s_gap", [P, 2, 4], F32, region)
            s_exp = sb("s_exp", [P, 2, 4], F32, region)
            den = sb("den", [P, 2, 4], F32, region)
            den_all = sb("den_all", [P, 2, 4], F32, region)
            den_inv = sb("den_inv", [P, 2, 4], F32, region)
        with ExitStack() as region:
            act_m = [sb("act_m_hi", [P, KB, T], F32R, region), sb("act_m_lo", [P, KB, T], F32R, region)]
            sq_sum = sb("sq_sum", [P, T], F32, region)
            rs_mlp = sb("rs_mlp", [P, T], F32, region)
        with ExitStack() as region:
            relu = sb("relu", [P, 2, T], F32, region)
            x_sq = sb("x_sq", [P, D_MODEL], F32, region)
            x_diag = sb("x_diag", [P, TT, P], F32, region)
            x_ss = sb("x_ss", [P, TT], F32, region)
            x_rs = sb("x_rs", [P, TT], F32, region)

        bank = [ctx.enter_context(nc.psum_tensor(f"bank{i}", [P, T], F32)) for i in range(8)]
        by_tt = [b[:].rearrange("p (t c) -> p t c", t=TT) for b in bank]
        by_dv = [b[:].rearrange("p (t c) -> p t c", c=DV) for b in bank]

        const_dma = sem("const_dma")
        const_pool = sem("const_pool")
        const_done = sem("const_done")
        cols_pe = sem("cols_pe")
        cols_dve = sem("cols_dve")
        raw_loaded = [sem(f"raw_loaded{i}") for i in range(RSLOTS)]
        w_hi_done = stream("w_hi_done", 0, w=1)
        w_lo_done = stream("w_lo_done", RSLOTS, w=1)
        tile_done = stream("tile_done", WSLOTS, t=1)
        evac = [stream(f"evac{i}", TILES // DBANKS, t=1) for i in range(DBANKS)]
        x_loaded = [sem(f"x_loaded{t}") for t in range(TT)]
        res_loaded = [sem(f"res_loaded{i}") for i in range(2)]
        stored = [sem(f"stored{i}") for i in range(2)]
        xn_stat = stream("xn_stat", 1, ss=TT, ln=1, rs=1)
        xn_diag = stream("xn_diag", 1, d=TT)
        xn_pe = stream("xn_pe", 1, t=KB)
        xn_hi = stream("xn_hi", 1, h=KB)
        xn_lo = stream("xn_lo", 1, l=KB)
        res_pe = stream("res_pe", 1, t=KB)
        res_copy = stream("res_copy", 1, c=KB)
        hm_hi = stream("hm_hi", 1, h=KB)
        hm_sq = stream("hm_sq", 1, s=KB)
        hm_lo = stream("hm_lo", 1, l=KB)
        hm_add = stream("hm_add", 1, a=KB - 1)
        hm_sum = stream("hm_sum", 1, s=1)
        hm_rs = stream("hm_rs", 1, ln=1, rs=1)
        lr_pe = stream("lr_pe", 1, t=1)
        lr_copy = stream("lr_copy", 1, t=1)
        al_pe = stream("al_pe", 1, z=1)
        al_act = stream("al_act", 1, abs=1, exp=1, ln=1)
        al_exp = stream("al_exp", 1, dec=1, e1=1, e3=1, e2=1)
        al_dve = stream("al_dve", 1, zmin=1, la=1, scan=TT, gap=1)
        v_pe = stream("v_pe", 1, t=2)
        v_copy = stream("v_copy", 1, t=2)
        g_tanh = stream("g_tanh", 1, t=2)
        ga_pe = stream("ga_pe", 1, ke=1, sc=1, kv=4, o=2, ot=2)
        ga_dve = stream("ga_dve", GLA_HEADS, ke=1, first=1, mask=TT, st=NCH, f=2)
        ga_lo = stream("ga_lo", 1, lo=2)
        ga_act = stream("ga_act", 1, ss=TT, ln=1, rs=1, o=TT, hi=2)
        sn_act = stream("sn_act", 1, sq=1, ln=1, rs=1)
        sn_pe = stream("sn_pe", 1, s=1)
        sn_dve = stream("sn_dve", 1, n=1)
        sn_hi = stream("sn_hi", 1, h=1)
        sn_lo = stream("sn_lo", 1, l=1)
        sk_hi = stream("sk_hi", 1, old=1)
        sk_lo = stream("sk_lo", 1, old=1, keep=1)
        sv_pe = stream("sv_pe", 1, t=1)
        sv_hi = stream("sv_hi", 1, h=1, old=1)
        sv_lo = stream("sv_lo", 1, l=1, old=1, keep=1)
        past_dve = stream("past_dve", 1, off=1)
        bias_act = stream("bias_act", 1, b=PAIR_HEADS)
        no_key = stream("no_key", 1, r=2)
        sc_pe = stream("sc_pe", 1, s=1)
        sm_dve = stream("sm_dve", 1, sink=1, ttr=4, neg=1, gap=1)
        sm_act = stream("sm_act", 1, p=4, sink=1)
        dn_dve = stream("dn_dve", 1, sum=1, inv=1, norm=4)
        pt_pe = stream("pt_pe", 2, t=2)
        pt_hi = stream("pt_hi", 1, h=2)
        pt_lo = stream("pt_lo", 1, l=2)
        pv_pe = stream("pv_pe", 1, o=1)
        so_hi = stream("so_hi", 1, h=1)
        so_lo = stream("so_lo", 1, l=1)
        mg_dve = stream("mg_dve", 1, mul=1, add=1)
        mg_act = stream("mg_act", 1, hi=1)
        up_relu = stream("up_relu", 1, r=1)
        up_sq = stream("up_sq", 1, sq=1, hi=1)
        fin_pe = stream("fin_pe", 1, t=KB)
        fin_act = stream("fin_act", 1, c=KB)

        def left(half, n, turn=0):
            return evac[n % DBANKS].at(half * (TILES // DBANKS) + turn * (TURN_TILES // DBANKS) + n // DBANKS, "t")

        def parts(n):
            return 2 if n in QUERY_TILES else 2 * PAIRS if N_BRANCH_B <= n < N_OUT else 1

        def raw_count(half, n, turn=0):
            of_half = sum(parts(i) for i in range(n % RSLOTS, TILES, RSLOTS))
            of_tile = sum(parts(i) for i in range(n % RSLOTS, n + 1, RSLOTS))
            return half * (16 * of_half) + turn * (16 * TURN_TILES // RSLOTS) + 16 * of_tile

        def x_rows(half):
            return (x[0].rearrange("(h t p) d -> h p t d", h=HALVES, p=P)[bass.ds(half, 1)]
                    .rearrange("h p t d -> p (h t) d"))

        swa_round = lambda half, p: half * PAIRS + p
        qk_round = lambda half, p, t: half * (PAIRS * 5) + (p * 5 + t)
        unit_round = lambda half, p, u: half * (PAIRS * UNITS) + (p * UNITS + u)
        block_round = lambda half, p, b: half * (PAIRS * TT) + (p * TT + b)
        gla_round = lambda half, h: half * GLA_HEADS + h
        up_round = lambda half, turn, j: half * (MLP_TURNS * KB) + turn * KB + j
        slopes = [2.0 ** (-8.0 * (h + 1) / SWA_HEADS) for h in range(SWA_HEADS)]

        w_in_v = w_in[0].rearrange("(k p) n -> p k n", p=P)
        block = ctx.enter_context(nc.Block())

        @block.sync
        def _(sp):
            def load(N, n, src):
                sp.wait_ge(w_lo_done.sem, w_lo_done.at(N - RSLOTS, "w"))
                for at, part in src if isinstance(src, list) else [((slice(None),) * 3, src)]:
                    sp.dma_start(w_raw[:, n % RSLOTS][at], part).then_inc(raw_loaded[n % RSLOTS], 16)

            def matrix(w, c):
                return w[0].rearrange("(k p) n -> p k n", p=P)[:, :, c * P:(c + 1) * P]

            for t in range(TT):
                sp.dma_start(x_tok[:, t:t + 1], x_rows(0)[:, t:t + 1]).then_inc(x_loaded[t], 16)
            for v, at in ((swa_q_norm, C_QN), (swa_k_norm, C_KN)):
                for side in range(2):
                    sp.dma_start(rows[at:at + 1, side * HD:(side + 1) * HD], v[0:1, :]).then_inc(const_dma, 16)
            sp.dma_start(sink_row[:], swa_sinks[0:1, :]).then_inc(const_dma, 16)
            sp.dma_start(wa_raw[:], w_in_v[:, :, GA:GA + RANK]).then_inc(const_dma, 16)
            for part in range(2):
                sp.dma_start(w_a2[part * RANK:(part + 1) * RANK, :], w_alpha2[0]).then_inc(const_dma, 16)
            with nc.sync.Fori(0, HALVES) as half:
                N = half * TILES
                cols_of = []
                for h in range(GLA_HEADS):
                    cols_of += [GG + h * DV, GG + h * DV + P, GV + h * DV, GV + h * DV + P, GQ + h * DK, GK + h * DK]
                for j, c in enumerate(cols_of):
                    load(N + j, j, w_in_v[:, :, c:c + P])
                for c in range(KB):
                    load(N + N_GATE_A + c, N_GATE_A + c, w_in_v[:, :, GATE_A + c * P:GATE_A + (c + 1) * P])
                for c in range(KB):
                    load(N + N_BRANCH_A + c, N_BRANCH_A + c, matrix(w_branch_gla, c))
                n = N_SWA
                for p in range(PAIRS):
                    for c in (SK + p * P, SV + p * P):
                        load(N + n, n, w_in_v[:, :, c:c + P])
                        n += 1
                    for j in range(4):
                        c = SQ + (p * PAIR_HEADS + j) * HD
                        d = c + PAIR_HEADS // 2 * HD
                        every = slice(None)
                        load(N + n, n, [((every, every, slice(0, HD)), w_in_v[:, :, c:c + HD]),
                                        ((every, every, slice(HD, P)), w_in_v[:, :, d:d + HD])])
                        n += 1
                for c in range(KB):
                    load(N + N_GATE_B + c, N_GATE_B + c, w_in_v[:, :, GATE_B + c * P:GATE_B + (c + 1) * P])
                for c in range(KB):
                    by_head = w_branch_swa[0].rearrange("(p r j d) n -> p r d j n", p=PAIRS, r=2, d=HD)
                    load(N + N_BRANCH_B + c, N_BRANCH_B + c,
                         [((slice(r * HD, r * HD + HD), slice(4 * p, 4 * p + 4)),
                           by_head[p, r, :, :, c * P:(c + 1) * P]) for p in range(PAIRS) for r in range(2)])
                for c in range(KB):
                    load(N + N_OUT + c, N_OUT + c, matrix(w_out, c))
                up_v = w_up[0].rearrange("(k p) n -> p k n", p=P)
                down_v = w_down[0].rearrange("(g k p) n -> g p k n", p=P, k=KB)

                def load_up(j, n, turn, up_turn):
                    load(half * TILES + turn * TURN_TILES + n, n,
                         up_v[:, :, bass.ds(up_turn * (KB * P) + j * P, P)])

                def load_down(c, n, turn):
                    w = down_v[bass.ds(turn, 1), :, :, c * P:(c + 1) * P]
                    load(half * TILES + turn * TURN_TILES + n, n, w.rearrange("g p k n -> p (g k) n"))

                for j in range(KB):
                    load_up(j, N_MLP + j, 0, 0)
                with nc.sync.Fori(0, MLP_TURNS - 1) as turn:
                    for c in range(KB):
                        load_down(c, N_MLP + KB + c, turn)
                    for j in range(KB):
                        load_up(j, N_MLP + 2 * KB + j, turn, turn + 1)
                for c in range(KB):
                    load_down(c, N_MLP + KB + c, MLP_TURNS - 1)
            for s in stored:
                sp.wait_ge(s, 16 * HALVES * KB // 2 + 16)

        @block.gpsimd
        def _(pool):
            count = [0]

            def link(ins):
                ins.then_inc(const_pool, 1)
                count[0] += 1
                pool.wait_ge(const_pool, count[0])

            g = nc.gpsimd
            w_lo_done.start(pool)
            link(g.memset(eps[:], EPS))
            link(g.memset(ident[:], 0.0))
            link(g.affine_select(out=ident[:], in_=ident[:], compare_op=ALU.not_equal, fill=1.0, base=0,
                                 pattern=[[-1, P]], channel_multiplier=1))
            assert count[0] == POOL_FIRST
            link(g.memset(ones[:], 1.0))
            link(g.memset(ones_hd[:], 0.0))
            link(g.memset(ones_hd[0:HD, 0:HD], 1.0))
            link(g.memset(ones_hd[HD:P, HD:P], 1.0))
            link(g.affine_select(out=causal_f[:], in_=ones_hd[:], compare_op=ALU.is_ge, fill=0.0, base=0,
                                 pattern=[[1, P]], channel_multiplier=-1))
            link(g.tensor_copy(causal[:], causal_f[:]))
            link(g.memset(restart[:], 1.0))
            link(g.memset(restart[:, 0:1], 0.0))
            link(g.memset(restart[:, CHUNK:CHUNK + 1], 0.0))
            link(g.iota(dist[:], pattern=[[1, 2 * P]], base=-P, channel_multiplier=-1,
                        allow_small_or_imprecise_dtypes=True))
            link(g.memset(no_past[:], NEG))
            link(g.memset(carry[:], 0.0))
            link(g.memset(masked[:], 0.0))
            link(g.memset(k_past[:], 0.0))
            link(g.memset(v_past[:], 0.0))
            assert count[0] == POOL_CONSTS
            with nc.gpsimd.Fori(0, HALVES * TILES // WSLOTS) as turn:
                for j in range(WSLOTS):
                    N = turn * WSLOTS + j
                    pool.wait_ge(w_hi_done.sem, w_hi_done.at(N, "w"))
                    g.tensor_tensor(w_lo[:, j], w_raw[:, j % RSLOTS], w_hi[:, j].bitcast(F32),
                                    ALU.subtract).then_inc(w_lo_done.sem, 1)

        @block.scalar
        def _(act):
            a = nc.scalar
            for s in ([xn_stat, xn_hi, res_copy, hm_hi, hm_sq, hm_rs, lr_copy, al_act, al_exp, g_tanh, ga_act, sn_act,
                                       bias_act, sm_act, sn_hi, sk_hi, sv_hi, pt_hi, so_hi, mg_act, up_sq, fin_act]):
                s.start(act)
            for s in stored:
                act.sem_inc(s, 16)
            a.preload_act_table_set(LN_EXP)
            gain_rows = [(norm_mix, C_MIX, 8), (norm_mlp, C_MLP, 8), (b_alpha, C_BA, 4), (gla_norm, C_GN, 2)]
            for v, at, n in gain_rows:
                act.dma_start(rows[at:at + n, :], v[0].rearrange("(r c) -> r c", r=n)).then_inc(const_dma, 16)

            def high(half, n):
                N = half * TILES + n
                act.wait_ge(raw_loaded[n % RSLOTS], raw_count(half, n))
                act.wait_ge(tile_done.sem, tile_done.at(N - WSLOTS, "t"))
                a.activation(w_hi[:, n % WSLOTS], w_raw[:, n % RSLOTS], ACT.Copy).then_inc(w_hi_done.sem, 1)

            def token_square(R, t):
                act.wait_ge(x_loaded[t], R * 16 + 16)
                if t > 0:
                    act.wait_ge(xn_stat.sem, xn_stat.at(R, "ss", t - 1))
                a.activation(x_sq[:], x_tok[:, t], ACT.Square, accum_out=x_ss[:, t:t + 1]).then_inc(xn_stat.sem, 1)

            def token_rs(R):
                act.wait_ge(xn_stat.sem, xn_stat.at(R, "ss"))
                a.activation(x_rs[:], x_ss[:], ACT.Ln, bias=eps[:], scale=1.0 / D_MODEL).then_inc(xn_stat.sem, 1)
                act.wait_ge(xn_stat.sem, xn_stat.at(R, "ln"))
                a.activation(x_rs[:], x_rs[:], ACT.Exp, scale=-0.5).then_inc(xn_stat.sem, 1)

            def x_high(R, k):
                act.wait_ge(xn_pe.sem, xn_pe.at(R, "t", k))
                a.activation(act_x[0][:, k], bank[4 + k % 4][:], ACT.Copy,
                             scale=cols[:, C_MIX + k:C_MIX + k + 1]).then_inc(xn_hi.sem, 1)

            for t in range(TT):
                token_square(0, t)
            act.wait_ge(const_pool, POOL_FIRST)
            token_rs(0)
            act.wait_ge(const_dma, CONST_DMAS * 16)
            act.wait_ge(const_pool, POOL_CONSTS)
            a.activation(wa_cols[:, :, 0], wa_raw[:], ACT.Copy).then_inc(const_done, 1)
            a.activation(wa_both[:, KB * 2 * RANK:], ones[:, 0:WA_COLS - KB * 2 * RANK],
                         ACT.Copy).then_inc(const_done, 1)
            a.activation(dist[:], dist[:], ACT.Abs).then_inc(const_done, 1)
            act.wait_ge(const_done, 3)
            a.activation(dist[:], dist[:], ACT.Copy, scale=-1.0).then_inc(const_done, 1)
            act.wait_ge(cols_dve, 2)
            for k in range(KB):
                x_high(0, k)

            with nc.scalar.Fori(0, HALVES) as half:
                for n in range(AHEAD):
                    high(half, n)
                act.wait_ge(lr_pe.sem, lr_pe.at(half, "t"))
                a.activation(a_low[:], bank[2][0:2 * RANK, :], ACT.Copy).then_inc(lr_copy.sem, 1)

                def alpha_ln(h):
                    R = gla_round(half, h)
                    act.wait_ge(al_pe.sem, al_pe.at(R, "z"))
                    if h > 0:
                        act.wait_ge(evac[(HEAD_TILES * h - 1) % DBANKS].sem, left(half, HEAD_TILES * h - 1))
                    ba = cols[:, C_BA + h:C_BA + h + 1]
                    a.activation(t_a[:], bank[2][:], ACT.Abs, bias=ba).then_inc(al_act.sem, 1)
                    act.wait_ge(al_act.sem, al_act.at(R, "abs"))
                    a.activation(t_a[:], t_a[:], ACT.Exp, scale=-1.0).then_inc(al_act.sem, 1)
                    a.preload_act_table_set(LN_EXP)
                    act.wait_ge(al_act.sem, al_act.at(R, "exp"))
                    a.activation(t_a[:], t_a[:], ACT.Ln, bias=ones[:, 0:1]).then_inc(al_act.sem, 1)

                def alpha_exp(h):
                    R = gla_round(half, h)
                    act.wait_ge(al_dve.sem, al_dve.at(R, "scan"))
                    total = cum[:].rearrange("p (c s) -> p c s", s=CHUNK)[:, :, CHUNK - 1]
                    a.activation(decay[:, h % 2], total, ACT.Exp, scale=1.0 / GLA_TAU).then_inc(al_exp.sem, 1)
                    a.activation(t_a[:], cum[:], ACT.Exp, scale=1.0 / GLA_TAU).then_inc(al_exp.sem, 1)
                    act.wait_ge(al_dve.sem, al_dve.at(R, "gap"))
                    a.activation(t_b[:], t_b[:], ACT.Exp, scale=-1.0 / GLA_TAU).then_inc(al_exp.sem, 1)
                    act.wait_ge(al_exp.sem, al_exp.at(R, "e1"))
                    a.activation(cum[:], cum[:], ACT.Exp, scale=-1.0 / GLA_TAU).then_inc(al_exp.sem, 1)

                def v_out(h, j):
                    n = HEAD_TILES * h + 2 + j
                    act.wait_ge(tile_done.sem, tile_done.at(half * TILES + n, "t"))
                    act.wait_ge(v_pe.sem, v_pe.at(gla_round(half, h) + j - 1, "t", 1 - j))
                    a.activation(vT[:], bank[n % DBANKS][:], ACT.Copy).then_inc(evac[n % DBANKS].sem, 1)

                def g_out(h, j):
                    n = HEAD_TILES * h + j
                    act.wait_ge(tile_done.sem, tile_done.at(half * TILES + n, "t"))
                    a.activation(silu[:, h % 2, j], bank[n % DBANKS][:], ACT.Tanh, scale=0.5).then_inc(g_tanh.sem, 1)

                def gla_norm_out(g):
                    R = gla_round(half, g)
                    if g == 0:
                        for s in stored:
                            act.wait_ge(s, half * (16 * KB // 2) + 16)
                    for b in range(TT):
                        act.wait_ge(ga_pe.sem, ga_pe.at(R, "o", b // 2))
                        a.activation(sq_ring[:, b // 2, b % 2 * DV:b % 2 * DV + DV], by_dv[4 + b // 2][:, b % 2], ACT.Square,
                                     accum_out=o_ss[:, b:b + 1]).then_inc(ga_act.sem, 1)
                    a.preload_act_table_set(LN_EXP)
                    act.wait_ge(ga_act.sem, ga_act.at(R, "ss"))
                    a.activation(o_rs[:], o_ss[:], ACT.Ln, bias=eps[:], scale=1.0 / DV).then_inc(ga_act.sem, 1)
                    act.wait_ge(ga_act.sem, ga_act.at(R, "ln"))
                    a.activation(o_rs[:], o_rs[:], ACT.Exp, scale=-0.5).then_inc(ga_act.sem, 1)
                    act.wait_ge(ga_act.sem, ga_act.at(R, "rs"))
                    for b in range(TT):
                        a.activation(o_tok[:, b], by_dv[4 + b // 2][:, b % 2], ACT.Copy,
                                     scale=o_rs[:, b:b + 1]).then_inc(ga_act.sem, 1)

                def gla_high_out(g):
                    R = gla_round(half, g)
                    for j in range(2):
                        act.wait_ge(ga_dve.sem, ga_dve.at(R, "f", j))
                        a.activation(act_o[0][:, 2 * g + j], bank[6 + j][:], ACT.Copy,
                                     scale=0.5).then_inc(ga_act.sem, 1)

                for h in range(GLA_HEADS + 1):
                    g = h - 1
                    for t in range(HEAD_TILES):
                        n = HEAD_TILES * h + t
                        high(half, n + AHEAD)
                        if h < GLA_HEADS:
                            if t == 1:
                                alpha_ln(h)
                            if t < 2:
                                g_out(h, t)
                            elif t < 4:
                                v_out(h, t - 2)
                            if t == 3:
                                alpha_exp(h)
                        else:
                            act.wait_ge(tile_done.sem, tile_done.at(half * TILES + n, "t"))
                            a.activation(gate[:, t], bank[n % DBANKS][:], ACT.Tanh,
                                         scale=0.5).then_inc(evac[n % DBANKS].sem, 1)
                        if g >= 0 and t == 3:
                            gla_norm_out(g)
                        if g >= 0 and t == 5:
                            gla_high_out(g)
                for c in range(HEAD_TILES, KB):
                    n = N_GATE_A + c
                    high(half, n + AHEAD)
                    act.wait_ge(tile_done.sem, tile_done.at(half * TILES + n, "t"))
                    a.activation(gate[:, c], bank[n % DBANKS][:], ACT.Tanh,
                                 scale=0.5).then_inc(evac[n % DBANKS].sem, 1)
                for c in range(KB):
                    high(half, N_BRANCH_A + c + AHEAD)

                def qk_norm(p, t, n):
                    R = qk_round(half, p, t)
                    act.wait_ge(tile_done.sem, tile_done.at(half * TILES + n, "t"))
                    if t >= 2 or p > 0:
                        act.wait_ge(sn_dve.sem, sn_dve.at(R - 2, "n"))
                    a.activation(qk_raw[:, (5 * p + t) % 2], bank[n % DBANKS][:],
                                 ACT.Copy).then_inc(evac[n % DBANKS].sem, 1)

                def qk_square(p, t, n):
                    R = qk_round(half, p, t)
                    slot = (5 * p + t) % 2
                    act.wait_ge(evac[(n) % DBANKS].sem, left(half, n))
                    act.wait_ge(sn_pe.sem, sn_pe.at(R - 1, "s"))
                    a.activation(sq_ring[:, 0], qk_raw[:, slot], ACT.Square).then_inc(sn_act.sem, 1)

                def qk_rs(p, t):
                    R = qk_round(half, p, t)
                    act.wait_ge(sn_pe.sem, sn_pe.at(R, "s"))
                    a.activation(bank[2][:], bank[2][:], ACT.Ln, bias=eps[:], scale=1.0 / HD).then_inc(sn_act.sem, 1)
                    act.wait_ge(sn_act.sem, sn_act.at(R, "ln"))
                    a.activation(bank[2][:], bank[2][:], ACT.Exp, scale=-0.5).then_inc(sn_act.sem, 1)

                def make_bias(p):
                    act.wait_ge(cols_dve, 6)
                    act.wait_ge(sm_dve.sem, sm_dve.at(unit_round(half, p, 0) - 1, "ttr"))
                    for i in range(PAIR_HEADS):
                        a.activation(bias[:, i], dist[:], ACT.Copy,
                                     scale=slopes[PAIR_HEADS * p + i] * HD ** 0.5).then_inc(bias_act.sem, 1)

                def qk_high(p, i):
                    act.wait_ge(sn_dve.sem, sn_dve.at(qk_round(half, p, i), "n"))
                    dst = k_win[0][:, p, P:] if i == 0 else act_o[0][:, 4 * p + i - 1]
                    a.activation(dst, bank[2][:], ACT.Copy).then_inc(sn_hi.sem, 1)
                    if i == 0:
                        a.activation(k_win[0][:, p, 0:P], k_past[:, p], ACT.Copy).then_inc(sk_hi.sem, 1)

                def v_high(p):
                    act.wait_ge(sv_pe.sem, sv_pe.at(swa_round(half, p), "t"))
                    a.activation(v_win[0][:, p, 1:], by_tt[2], ACT.Copy).then_inc(sv_hi.sem, 1)
                    a.activation(v_win[0][:, p, 0], v_past[:, p], ACT.Copy).then_inc(sv_hi.sem, 1)

                def soft_exp(p, u):
                    R = unit_round(half, p, u)
                    act.wait_ge(sm_dve.sem, sm_dve.at(R, "neg"))
                    if u >= 2 or p > 0:
                        act.wait_ge(dn_dve.sem, dn_dve.at(R - 2, "inv"))
                    for i in range(4):
                        a.activation(prob[:, u % 2, i], prob[:, u % 2, i], ACT.Exp, bias=m_neg[:, u % 2, i:i + 1],
                                     accum_out=den[:, u % 2, i:i + 1]).then_inc(sm_act.sem, 1)
                    act.wait_ge(sm_dve.sem, sm_dve.at(R, "gap"))
                    a.activation(s_exp[:, u % 2], s_gap[:, u % 2], ACT.Exp).then_inc(sm_act.sem, 1)

                def prob_high(p, u):
                    R = unit_round(half, p, u)
                    act.wait_ge(pv_pe.sem, pv_pe.at(R - 1, "o"))
                    for r in range(2):
                        act.wait_ge(pt_pe.sem, pt_pe.at(R, "t", r))
                        a.activation(probT[0][:, r].rearrange("q k c -> q (k c)"), bank[5 + r][:],
                                     ACT.Copy).then_inc(pt_hi.sem, 1)

                def swa_high_out(p, b):
                    act.wait_ge(pv_pe.sem, pv_pe.at(unit_round(half, p, 2 * b + 1), "o"))
                    a.activation(act_o[0][:, 4 * p:4 * p + 4, b * P:(b + 1) * P], by_tt[7],
                                 ACT.Copy).then_inc(so_hi.sem, 1)

                def swa_slot(p, s):
                    if s % 2 == 0 and 0 <= (s - 4) // 2 < TT:
                        swa_high_out(p, (s - 4) // 2)
                    if 2 <= s <= UNITS + 1:
                        prob_high(p, s - 2)
                    if s < UNITS:
                        soft_exp(p, s)

                a.preload_act_table_set(LN_EXP)
                for p in range(PAIRS):
                    R = swa_round(half, p)
                    for t in range(HEAD_TILES):
                        n = N_SWA + p * HEAD_TILES + t
                        if p == 0:
                            high(half, n + AHEAD)
                        if t == 0 and p > 0:
                            qk_rs(p - 1, 4)
                        if t == 1 or t > 2:
                            qk_rs(p, 0 if t == 1 else t - 2)
                        if t == 0 and p > 0:
                            qk_high(p - 1, 4)
                        if p == 0 and (t == 1 or t > 2):
                            qk_high(p, 0 if t == 1 else t - 2)
                        if t == 2:
                            v_high(p)
                        if p > 0:
                            if t > 0:
                                swa_slot(p - 1, 2 * t - 1)
                            high(half, n + AHEAD)
                        if p > 0 and (t == 1 or t > 2):
                            qk_high(p, 0 if t == 1 else t - 2)
                        if t == 1:
                            act.wait_ge(tile_done.sem, tile_done.at(half * TILES + n, "t"))
                            act.wait_ge(sv_pe.sem, sv_pe.at(R - 1, "t"))
                            a.activation(svT, bank[n % DBANKS][:], ACT.Copy).then_inc(evac[n % DBANKS].sem, 1)
                        else:
                            i = 0 if t == 0 else t - 1
                            qk_norm(p, i, n)
                            qk_square(p, i, n)
                        if p > 0:
                            swa_slot(p - 1, 2 * t)
                        if t == 4:
                            make_bias(p)
                for c in range(KB):
                    n = N_GATE_B + c
                    if c == 0:
                        qk_rs(PAIRS - 1, 4)
                        qk_high(PAIRS - 1, 4)
                        a.preload_act_table_set(EXP_TANH)
                    if c > 0:
                        swa_slot(PAIRS - 1, 2 * c - 1)
                    high(half, n + AHEAD)
                    act.wait_ge(tile_done.sem, tile_done.at(half * TILES + n, "t"))
                    if c == 0:
                        act.wait_ge(fin_pe.sem, fin_pe.at(half - 1, "t"))
                    a.activation(resid[:, c], bank[n % DBANKS][:], ACT.Tanh,
                                 scale=0.5).then_inc(evac[n % DBANKS].sem, 1)
                    swa_slot(PAIRS - 1, 2 * c)
                for c in range(KB):
                    n = N_BRANCH_B + c
                    high(half, n + AHEAD)
                    act.wait_ge(mg_dve.sem, mg_dve.at(half * KB + c, "add"))
                    a.activation(act_m[0][:, c], bank[n % DBANKS][:], ACT.Copy, scale=0.5).then_inc(mg_act.sem, 1)
                    if c % 4 == 3:
                        i = c // 4
                        act.wait_ge(mg_dve.sem, mg_dve.at(half * KB + c, "add"))
                        act.dma_start(gate[:, i * TT:(i + 1) * TT],
                                      x_rows(half)[:, :, i * T:(i + 1) * T]).then_inc(res_loaded[i], 16)

                a.preload_act_table_set(LN_EXP)

                def high_mlp(n, turn):
                    N = half * TILES + turn * TURN_TILES + n
                    act.wait_ge(raw_loaded[n % RSLOTS], raw_count(half, n, turn))
                    act.wait_ge(tile_done.sem, tile_done.at(N - WSLOTS, "t"))
                    a.activation(w_hi[:, n % WSLOTS], w_raw[:, n % RSLOTS], ACT.Copy).then_inc(w_hi_done.sem, 1)

                for c in range(KB):
                    high_mlp(N_OUT + c + AHEAD, 0)
                    act.wait_ge(res_pe.sem, res_pe.at(half, "t", c))
                    a.activation(resid[:, c], bank[2 + c % 2][:], ACT.Copy).then_inc(res_copy.sem, 1)
                    act.wait_ge(evac[(N_OUT + c) % DBANKS].sem, left(half, N_OUT + c))
                    a.activation(act_x[0][:, c], resid[:, c], ACT.Copy,
                                 scale=cols[:, C_MLP + c:C_MLP + c + 1]).then_inc(hm_hi.sem, 1)
                    if c > 2:
                        act.wait_ge(hm_add.sem, hm_add.at(half, "a", c - 3))
                    a.activation(sq_sum[:] if c == 0 else sq_ring[:, c % 2], resid[:, c],
                                 ACT.Square).then_inc(hm_sq.sem, 1)

                act.wait_ge(res_pe.sem, res_pe.at(half, "t"))
                for t in range(TT):
                    act.dma_start(x_tok[:, t:t + 1],
                                  x_rows(HALVES - 1 - half)[:, t:t + 1]).then_inc(x_loaded[t], 16)

                def up_out(j, turn):
                    R = up_round(half, turn, j)
                    act.wait_ge(up_relu.sem, up_relu.at(R, "r"))
                    a.activation(bank[j % DBANKS][:], relu[:, j % 2], ACT.Square).then_inc(up_sq.sem, 1)
                    a.activation(act_o[0][:, j], relu[:, j % 2], ACT.Square).then_inc(up_sq.sem, 1)

                for j in range(KB):
                    high_mlp(N_MLP + j + AHEAD, 0)
                    if j == 0:
                        act.wait_ge(hm_sum.sem, hm_sum.at(half, "s"))
                        a.activation(rs_mlp[:], bank[6][:], ACT.Ln, bias=eps[:],
                                     scale=1.0 / D_MODEL).then_inc(hm_rs.sem, 1)
                        act.wait_ge(hm_rs.sem, hm_rs.at(half, "ln"))
                        a.activation(rs_mlp[:], rs_mlp[:], ACT.Exp, scale=-0.5).then_inc(hm_rs.sem, 1)
                    up_out(j, 0)
                    if j >= KB - TT:
                        token_square(half + 1, j - (KB - TT))
                token_rs(half + 1)
                with nc.scalar.Fori(0, MLP_TURNS - 1) as turn:
                    for c in range(KB):
                        high_mlp(N_MLP + KB + c + AHEAD, turn)
                    for j in range(KB):
                        high_mlp(N_MLP + 2 * KB + j + AHEAD, turn)
                        up_out(j, turn + 1)

                def final_copy(c):
                    act.wait_ge(fin_pe.sem, fin_pe.at(half, "t", c))
                    act.wait_ge(stored[c % 2], half * (16 * KB // 2) + 16 * (c // 2) + 16)
                    a.activation(o_stage[:, c % 2], by_tt[2 + c % 2], ACT.Copy).then_inc(fin_act.sem, 1)

                def store(c):
                    act.wait_ge(fin_act.sem, fin_act.at(half, "c", c))
                    act.dma_start(out[0].rearrange("(h t p) d -> h p t d", h=HALVES, p=P)
                                  [bass.ds(half, 1), :, :, c * P:(c + 1) * P].rearrange("h p t d -> p (h t) d"),
                                  o_stage[:, c % 2]).then_inc(stored[c % 2], 16)

                for c in range(KB):
                    if c + AHEAD < KB:
                        high_mlp(N_MLP + KB + c + AHEAD, MLP_TURNS - 1)
                    if c > 1:
                        store(c - 2)
                    x_high(half + 1, c)
                    if c > 0:
                        final_copy(c - 1)
                store(KB - 2)
                final_copy(KB - 1)
                store(KB - 1)

        @block.vector
        def _(dve):
            v = nc.vector
            for s in (evac + [xn_diag, xn_lo, hm_lo, hm_add, up_relu, al_dve, v_copy, ga_dve, ga_lo, sn_dve, sn_lo, sk_lo,
                              sv_lo, past_dve, no_key, sm_dve, dn_dve, pt_lo, so_lo, mg_dve]):
                s.start(dve)
            def token_scale(R, t):
                if t == 0:
                    dve.wait_ge(xn_stat.sem, xn_stat.at(R, "rs"))
                v.tensor_scalar(x_diag[:, t], ident[:], x_rs[:, t:t + 1], None, ALU.mult).then_inc(xn_diag.sem, 1)

            def x_low(R, k):
                dve.wait_ge(xn_hi.sem, xn_hi.at(R, "h", k))
                v.scalar_tensor_tensor(act_x[1][:, k], bank[4 + k % 4][:], cols[:, C_MIX + k:C_MIX + k + 1],
                                       act_x[0][:, k].bitcast(F32), ALU.mult, ALU.subtract).then_inc(xn_lo.sem, 1)

            dve.wait_ge(cols_pe, 2)
            v.tensor_copy(cols[:], bank[2][:, 0:C_ALL]).then_inc(cols_dve, 1)
            for p in range(PAIRS):
                of_pair = slice(p * PAIR_HEADS, (p + 1) * PAIR_HEADS)
                v.tensor_copy(sink[:, of_pair].rearrange("q (j r e) -> q j r e", j=2, r=2),
                              bank[3][:, of_pair].rearrange("q (r j e) -> q j r e", r=2, j=2)).then_inc(cols_dve, 1)
            for t in range(TT):
                token_scale(0, t)
            dve.wait_ge(const_done, 2)
            v.tensor_tensor(wa_cols[:, :, 1], wa_raw[:], wa_cols[:, :, 0].bitcast(F32),
                            ALU.subtract).then_inc(cols_dve, 1)
            dve.wait_ge(cols_dve, 3)
            for k in range(KB):
                x_low(0, k)
            dve.wait_ge(const_done, 4)
            v.memset(dist[0:CHUNK, P + CHUNK:], NEG).then_inc(cols_dve, 1)
            v.memset(dist[CHUNK:P, 0:CHUNK], NEG).then_inc(cols_dve, 1)
            v.tensor_scalar(sink_neg[:], sink[:], -1.0, None, ALU.mult).then_inc(cols_dve, 1)
            dve.wait_ge(cols_dve, 7)

            with nc.vector.Fori(0, HALVES) as half:

                def alpha(h):
                    R = gla_round(half, h)
                    dve.wait_ge(al_act.sem, al_act.at(R, "abs"))
                    v.tensor_scalar(t_b[:], bank[2][:], cols[:, C_BA + h:C_BA + h + 1], 0.0, ALU.add,
                                    ALU.min).then_inc(al_dve.sem, 1)
                    dve.wait_ge(al_act.sem, al_act.at(R, "ln"))
                    dve.wait_ge(al_dve.sem, al_dve.at(R, "zmin"))
                    v.tensor_tensor(t_b[:], t_b[:], t_a[:], ALU.subtract).then_inc(al_dve.sem, 1)
                    dve.wait_ge(al_dve.sem, al_dve.at(R, "la"))
                    for b in range(TT):
                        v.tensor_tensor_scan(cum[:, b * P:(b + 1) * P], restart[:], t_b[:, b * P:(b + 1) * P], 0.0,
                                             ALU.mult, ALU.add).then_inc(al_dve.sem, 1)
                    dve.wait_ge(al_dve.sem, al_dve.at(R, "scan"))
                    by_chunk = cum[:].rearrange("p (c s) -> p c s", s=CHUNK)
                    total = by_chunk[:, :, CHUNK - 1:CHUNK].to_broadcast([P, NCH, CHUNK])
                    v.tensor_tensor(t_b[:].rearrange("p (c s) -> p c s", s=CHUNK), by_chunk, total,
                                    ALU.subtract).then_inc(al_dve.sem, 1)

                def v_tokens(h, j):
                    dve.wait_ge(v_pe.sem, v_pe.at(gla_round(half, h), "t", j))
                    v.tensor_copy(v_tok[:, :, j * P:(j + 1) * P], by_tt[3]).then_inc(v_copy.sem, 1)

                def silu_out(h, j):
                    n = HEAD_TILES * h + j
                    dve.wait_ge(g_tanh.sem, g_tanh.at(gla_round(half, h), "t", j))
                    v.scalar_tensor_tensor(silu[:, h % 2, j], silu[:, h % 2, j], 1.0, bank[n % DBANKS][:],
                                           ALU.add, ALU.mult).then_inc(evac[n % DBANKS].sem, 1)

                def q_out(h):
                    n = HEAD_TILES * h + 4
                    dve.wait_ge(tile_done.sem, tile_done.at(half * TILES + n, "t"))
                    dve.wait_ge(al_exp.sem, al_exp.at(gla_round(half, h), "e1"))
                    v.scalar_tensor_tensor(q_dec[:], bank[n % DBANKS][:], DK ** -0.5, t_a[:], ALU.mult,
                                           ALU.mult).then_inc(evac[n % DBANKS].sem, 1)

                def k_out(h):
                    n = HEAD_TILES * h + 5
                    dve.wait_ge(tile_done.sem, tile_done.at(half * TILES + n, "t"))
                    dve.wait_ge(al_exp.sem, al_exp.at(gla_round(half, h), "e2"))
                    v.tensor_tensor(k_dec[:], bank[n % DBANKS][:], cum[:], ALU.mult)
                    v.tensor_tensor(k_end[:], bank[n % DBANKS][:], t_b[:],
                                    ALU.mult).then_inc(evac[n % DBANKS].sem, 1)

                def states(g, first, last):
                    R = gla_round(half, g)
                    for c in range(first, last):
                        if c % 4 == 0:
                            dve.wait_ge(ga_pe.sem, ga_pe.at(R, "kv", c // 2 + 1))
                        if c == 0:
                            dve.wait_ge(ga_dve.sem, ga_dve.at(R, "first"))
                        else:
                            dve.wait_ge(ga_dve.sem, ga_dve.at(R, "st", c - 1))
                        dst = state[:, c + 1] if c + 1 < NCH else carry[:, g]
                        v.scalar_tensor_tensor(dst, state[:, c], decay[:, g % 2, c:c + 1],
                                               by_dv[6 + c % 2][:, c // 2 % 2], ALU.mult,
                                               ALU.add).then_inc(ga_dve.sem, 1)

                def gla_step(g, t):
                    R = gla_round(half, g)
                    if t == 0:
                        dve.wait_ge(ga_pe.sem, ga_pe.at(R, "ke"))
                        v.tensor_copy(ke_tok[:], by_tt[4]).then_inc(ga_dve.sem, 1)
                        dve.wait_ge(ga_dve.sem, ga_dve.at(R - GLA_HEADS, "st"))
                        dve.wait_ge(ga_pe.sem, ga_pe.at(R, "sc"))
                        v.tensor_copy(state[:, 0], carry[:, g]).then_inc(ga_dve.sem, 1)
                        for b in range(TT):
                            v.copy_predicated(masked[:, b], causal[:], by_tt[5][:, b]).then_inc(ga_dve.sem, 1)
                    if t == 1:
                        states(g, 0, 4)
                    if t == 2:
                        states(g, 4, NCH)
                    if t == 5:
                        for j in range(2):
                            dve.wait_ge(ga_pe.sem, ga_pe.at(R, "ot", j))
                            v.scalar_tensor_tensor(bank[6 + j][:], bank[6 + j][:], cols[:, C_GN + j:C_GN + j + 1],
                                                   silu[:, g % 2, j], ALU.mult, ALU.mult).then_inc(ga_dve.sem, 1)
                    if t == 6:
                        for j in range(2):
                            dve.wait_ge(ga_act.sem, ga_act.at(R, "hi", j))
                            v.scalar_tensor_tensor(act_o[1][:, 2 * g + j], bank[6 + j][:], 0.5,
                                                   act_o[0][:, 2 * g + j].bitcast(F32), ALU.mult,
                                                   ALU.subtract).then_inc(ga_lo.sem, 1)

                for h in range(GLA_HEADS + 1):
                    for t in range(HEAD_TILES):
                        if h > 0:
                            if t == 5 and h < GLA_HEADS:
                                dve.wait_ge(evac[(HEAD_TILES * h + 1) % DBANKS].sem, left(half, HEAD_TILES * h + 1))
                            elif t == 5:
                                dve.wait_ge(evac[(HEAD_TILES * (h - 1) + 5) % DBANKS].sem, left(half, HEAD_TILES * (h - 1) + 5))
                            gla_step(h - 1, t)
                        if h < GLA_HEADS:
                            if t < 2:
                                silu_out(h, t)
                            if t == 2:
                                alpha(h)
                            if t == 3 or t == 4:
                                v_tokens(h, t - 3)
                            if t == 4:
                                q_out(h)
                            if t == 5:
                                k_out(h)
                        if h > 0 and t == 5:
                            gla_step(h - 1, 6)
                for c in range(KB):
                    n = N_BRANCH_A + c
                    dve.wait_ge(tile_done.sem, tile_done.at(half * TILES + n, "t"))
                    v.scalar_tensor_tensor(gate[:, c], gate[:, c], 1.0, bank[n % DBANKS][:], ALU.add,
                                           ALU.mult).then_inc(evac[n % DBANKS].sem, 1)

                def qk_out(p, i):
                    R = qk_round(half, p, i)
                    dve.wait_ge(sn_act.sem, sn_act.at(R, "rs"))
                    gain = C_KN if i == 0 else C_QN
                    v.scalar_tensor_tensor(bank[2][:], qk_raw[:, (5 * p + i) % 2], cols[:, gain:gain + 1],
                                           bank[2][:], ALU.mult, ALU.mult).then_inc(sn_dve.sem, 1)

                def qk_low(p, i):
                    dve.wait_ge(sn_hi.sem, sn_hi.at(qk_round(half, p, i), "h"))
                    hi, lo = ((w[:, p, P:] if i == 0 else o[:, 4 * p + i - 1]) for w, o in zip(k_win, act_o))
                    v.tensor_tensor(lo, bank[2][:], hi.bitcast(F32), ALU.subtract).then_inc(sn_lo.sem, 1)
                    if i == 0:
                        R = swa_round(half, p)
                        dve.wait_ge(sk_hi.sem, sk_hi.at(R, "old"))
                        v.tensor_tensor(k_win[1][:, p, 0:P], k_past[:, p], k_win[0][:, p, 0:P].bitcast(F32),
                                        ALU.subtract).then_inc(sk_lo.sem, 1)
                        dve.wait_ge(sk_lo.sem, sk_lo.at(R, "old"))
                        v.tensor_copy(k_past[:, p], bank[2][:, T - P:]).then_inc(sk_lo.sem, 1)

                def swa_slot(p, s, between=None):
                    def normalize():
                        u = s - 1
                        R = unit_round(half, p, u)
                        dve.wait_ge(sm_act.sem, sm_act.at(R, "sink"))
                        v.tensor_tensor(den_all[:, u % 2], den[:, u % 2], s_exp[:, u % 2],
                                        ALU.add).then_inc(dn_dve.sem, 1)
                        dve.wait_ge(dn_dve.sem, dn_dve.at(R, "sum"))
                        v.reciprocal(den_inv[:, u % 2], den_all[:, u % 2]).then_inc(dn_dve.sem, 1)
                        dve.wait_ge(dn_dve.sem, dn_dve.at(R, "inv"))
                        for i in range(4):
                            v.tensor_scalar(prob[:, u % 2, i], prob[:, u % 2, i], den_inv[:, u % 2, i:i + 1], None,
                                            ALU.mult).then_inc(dn_dve.sem, 1)

                    if 2 <= s <= UNITS:
                        normalize()
                    if s == 0:
                        dve.wait_ge(bias_act.sem, bias_act.at(swa_round(half, p), "b"))
                        dve.wait_ge(past_dve.sem, past_dve.at(half - 1, "off"))
                    if s < UNITS:
                        b, jj = s // 2, s % 2
                        R = unit_round(half, p, s)
                        dve.wait_ge(sc_pe.sem, sc_pe.at(R, "s"))
                        if b == 0:
                            M = swa_round(half, p) * 2 + jj
                            for r in range(2):
                                old = bank[3 + r][:].rearrange("q (e k) -> q e k", e=2)[:, :, 0:P]
                                v.tensor_scalar(old, old, no_past[:], None, ALU.add).then_inc(no_key.sem, 1)
                            dve.wait_ge(no_key.sem, no_key.at(M, "r"))
                        dve.wait_ge(pt_pe.sem, pt_pe.at(R - 2, "t"))
                        of_unit = slice((p * 2 + jj) * 4, (p * 2 + jj) * 4 + 4)
                        v.tensor_copy(m_neg[:, s % 2], sink_neg[:, of_unit]).then_inc(sm_dve.sem, 1)
                        for i in range(4):
                            r, e = i // 2, i % 2
                            v.tensor_tensor_reduce(prob[:, s % 2, i], bank[3 + r][:, e * 2 * P:(e + 1) * 2 * P],
                                                   bias[:, 4 * r + 2 * jj + e], HD ** -0.5, -3.0e38, ALU.add,
                                                   ALU.max, mx[:, s % 2, i:i + 1]).then_inc(sm_dve.sem, 1)
                        dve.wait_ge(sm_dve.sem, sm_dve.at(R, "ttr"))
                        v.scalar_tensor_tensor(m_neg[:, s % 2], mx[:, s % 2], -1.0, m_neg[:, s % 2], ALU.mult,
                                               ALU.min).then_inc(sm_dve.sem, 1)
                        dve.wait_ge(sm_dve.sem, sm_dve.at(R, "neg"))
                        v.tensor_tensor(s_gap[:, s % 2], sink[:, of_unit], m_neg[:, s % 2],
                                        ALU.add).then_inc(sm_dve.sem, 1)
                    if s == 1:
                        normalize()
                    if between:
                        between()
                    if s % 2 == 0 and 0 <= (s - 4) // 2 < TT:
                        b = (s - 4) // 2
                        dve.wait_ge(so_hi.sem, so_hi.at(block_round(half, p, b), "h"))
                        at = (slice(None), slice(4 * p, 4 * p + 4), slice(b * P, (b + 1) * P))
                        v.tensor_tensor(act_o[1][at], by_tt[7], act_o[0][at].bitcast(F32),
                                        ALU.subtract).then_inc(so_lo.sem, 1)
                    if 2 <= s <= UNITS + 1:
                        R = unit_round(half, p, s - 2)
                        for r in range(2):
                            dve.wait_ge(pt_hi.sem, pt_hi.at(R, "h", r))
                            v.tensor_tensor(probT[1][:, r].rearrange("q k c -> q (k c)"), bank[5 + r][:],
                                            probT[0][:, r].rearrange("q k c -> q (k c)").bitcast(F32),
                                            ALU.subtract).then_inc(pt_lo.sem, 1)
                for p in range(PAIRS):
                    for t in range(HEAD_TILES):
                        def norm_out():
                            if t == 0 and p > 0:
                                qk_out(p - 1, 4)
                            if t == 1 or t > 2:
                                qk_out(p, 0 if t == 1 else t - 2)
                            if t == 2:
                                R = swa_round(half, p)
                                dve.wait_ge(sv_hi.sem, sv_hi.at(R, "old"))
                                v.tensor_tensor(v_win[1][:, p, 1:], by_tt[2], v_win[0][:, p, 1:].bitcast(F32),
                                                ALU.subtract).then_inc(sv_lo.sem, 1)
                                v.tensor_tensor(v_win[1][:, p, 0], v_past[:, p], v_win[0][:, p, 0].bitcast(F32),
                                                ALU.subtract).then_inc(sv_lo.sem, 1)
                                dve.wait_ge(sv_lo.sem, sv_lo.at(R, "old"))
                                v.tensor_copy(v_past[:, p], by_tt[2][:, TT - 1]).then_inc(sv_lo.sem, 1)

                        def low_out():
                            if t == 0 and p > 0:
                                qk_low(p - 1, 4)
                            if t == 1 or t > 2:
                                qk_low(p, 0 if t == 1 else t - 2)

                        if p == 0 or t == 0:
                            norm_out()
                            low_out()
                        if p > 0:
                            if t > 0:
                                swa_slot(p - 1, 2 * t - 1, norm_out)
                            swa_slot(p - 1, 2 * t, low_out if t > 0 else None)
                qk_out(PAIRS - 1, 4)
                qk_low(PAIRS - 1, 4)
                for s in range(UNITS + 3):
                    swa_slot(PAIRS - 1, s)
                v.memset(no_past[:], 0.0).then_inc(past_dve.sem, 1)

                for c in range(KB):
                    n = N_BRANCH_B + c
                    b = bank[n % DBANKS][:]
                    R = half * KB + c
                    dve.wait_ge(tile_done.sem, tile_done.at(half * TILES + n, "t"))
                    v.scalar_tensor_tensor(b, resid[:, c], 1.0, b, ALU.add, ALU.mult).then_inc(mg_dve.sem, 1)
                    dve.wait_ge(mg_dve.sem, mg_dve.at(R, "mul"))
                    v.tensor_tensor(b, b, gate[:, c], ALU.add).then_inc(mg_dve.sem, 1)
                    dve.wait_ge(mg_act.sem, mg_act.at(R, "hi"))
                    v.scalar_tensor_tensor(act_m[1][:, c], b, 0.5, act_m[0][:, c].bitcast(F32), ALU.mult,
                                           ALU.subtract).then_inc(evac[n % DBANKS].sem, 1)
                for c in range(KB):
                    n = N_OUT + c
                    dve.wait_ge(res_copy.sem, res_copy.at(half, "c", c))
                    dve.wait_ge(tile_done.sem, tile_done.at(half * TILES + n, "t"))
                    v.tensor_tensor(resid[:, c], bank[n % DBANKS][:], resid[:, c],
                                    ALU.add).then_inc(evac[n % DBANKS].sem, 1)
                    dve.wait_ge(hm_hi.sem, hm_hi.at(half, "h", c))
                    v.scalar_tensor_tensor(act_x[1][:, c], resid[:, c], cols[:, C_MLP + c:C_MLP + c + 1],
                                           act_x[0][:, c].bitcast(F32), ALU.mult,
                                           ALU.subtract).then_inc(hm_lo.sem, 1)
                    if c > 0:
                        dve.wait_ge(hm_sq.sem, hm_sq.at(half, "s", c))
                        if c > 1:
                            dve.wait_ge(hm_add.sem, hm_add.at(half, "a", c - 2))
                        v.tensor_tensor(sq_sum[:], sq_sum[:], sq_ring[:, c % 2], ALU.add).then_inc(hm_add.sem, 1)

                def up_out(j, n, turn, up_turn):
                    R = up_round(half, up_turn, j)
                    dve.wait_ge(tile_done.sem, tile_done.at(half * TILES + turn * TURN_TILES + n, "t"))
                    v.scalar_tensor_tensor(relu[:, j % 2], bank[n % DBANKS][:], 0.0, rs_mlp[:], ALU.max,
                                           ALU.mult).then_inc(up_relu.sem, 1)
                    dve.wait_ge(up_sq.sem, up_sq.at(R, "hi"))
                    v.tensor_tensor(act_o[1][:, j], bank[n % DBANKS][:], act_o[0][:, j].bitcast(F32),
                                    ALU.subtract).then_inc(evac[n % DBANKS].sem, 1)

                def down_out(c, turn):
                    n = N_MLP + KB + c
                    dve.wait_ge(tile_done.sem, tile_done.at(half * TILES + turn * TURN_TILES + n, "t"))
                    dve.wait_ge(evac[(n - 1) % DBANKS].sem, left(half, n - 1, turn))
                    v.tensor_tensor(resid[:, c], bank[n % DBANKS][:], resid[:, c],
                                    ALU.add).then_inc(evac[n % DBANKS].sem, 1)

                dve.wait_ge(hm_rs.sem, hm_rs.at(half, "rs"))
                for j in range(KB):
                    up_out(j, N_MLP + j, 0, 0)
                for t in range(TT):
                    token_scale(half + 1, t)
                with nc.vector.Fori(0, MLP_TURNS - 1) as turn:
                    for c in range(KB):
                        down_out(c, turn)
                    for j in range(KB):
                        up_out(j, N_MLP + 2 * KB + j, turn, turn + 1)
                for c in range(KB):
                    x_low(half + 1, c)
                    down_out(c, MLP_TURNS - 1)

        @block.tensor
        def _(pe):
            t_ = nc.tensor
            for s in (tile_done, xn_pe, res_pe, hm_sum, lr_pe, al_pe, v_pe, ga_pe, sn_pe, sv_pe, sc_pe, pt_pe, pv_pe,
                      fin_pe):
                s.start(pe)
            def dense(half, n, src, mid=None, turn=0, ready=None):
                N = half * TILES + turn * TURN_TILES + n
                pe.wait_ge(w_lo_done.sem, w_lo_done.at(N, "w"))
                pe.wait_ge(evac[n % DBANKS].sem, left(half, n - DBANKS, turn))
                hi, lo = w_hi[:, n % WSLOTS], w_lo[:, n % WSLOTS]
                o = bank[n % DBANKS][:]
                for k in range(KB):
                    if k == KB // 2 and mid:
                        mid()
                    if ready:
                        ready(k)
                    t_.matmul(o, hi[:, k], src[0][:, k], start=k == 0, stop=False)
                    t_.matmul(o, lo[:, k], src[0][:, k], start=False, stop=False)
                    last = t_.matmul(o, hi[:, k], src[1][:, k], start=False, stop=k == KB - 1)
                last.then_inc(tile_done.sem, 1)

            def transposes(dst, src_of, n=TT):
                for b in range(n):
                    last = t_.transpose(dst[:, b], src_of(b), ident[:])
                return last

            def x_scaled(R, k):
                if k == 0:
                    pe.wait_ge(xn_diag.sem, xn_diag.at(R, "d"))
                if k >= 4:
                    pe.wait_ge(xn_lo.sem, xn_lo.at(R, "l", k - 4))
                for b in range(TT):
                    last = t_.matmul(by_tt[4 + k % 4][:, b], x_tok[:, b, k * P:(k + 1) * P], x_diag[:, b],
                                     start=True, stop=True)
                last.then_inc(xn_pe.sem, 1)

            pe.wait_ge(const_pool, POOL_CONSTS)
            pe.wait_ge(const_dma, CONST_DMAS * 16)
            t_.transpose(bank[2][:, 0:C_ALL], rows[:], ident[0:C_ALL, 0:C_ALL]).then_inc(cols_pe, 1)
            t_.matmul(bank[3][:, 0:SWA_HEADS], ones[0:1, :], sink_row[:], start=True,
                      stop=True).then_inc(cols_pe, 1)
            for k in range(KB):
                x_scaled(0, k)

            with nc.tensor.Fori(0, HALVES) as half:
                pe.wait_ge(cols_dve, 4)
                pe.wait_ge(fin_act.sem, fin_act.at(half - 1, "c", KB - 2))
                for k in range(KB):
                    cut = slice(k * 2 * RANK, k * 2 * RANK + P)
                    pe.wait_ge(xn_lo.sem, xn_lo.at(half, "l", k))
                    t_.matmul(bank[2][:], wa_both[:, cut], act_x[0][:, k], start=k == 0, stop=False)
                    last = t_.matmul(bank[2][:], wa_both[:, cut], act_x[1][:, k], start=False, stop=k == KB - 1)
                last.then_inc(lr_pe.sem, 1)

                def alpha(h):
                    R = gla_round(half, h)
                    if h == 0:
                        pe.wait_ge(lr_copy.sem, lr_copy.at(half, "t"))
                    else:
                        pe.wait_ge(al_dve.sem, al_dve.at(R - 1, "zmin"))
                    t_.matmul(bank[2][:], w_a2[:, h * DK:(h + 1) * DK], a_low[:], start=True,
                              stop=True).then_inc(al_pe.sem, 1)

                def v_turn(h, j):
                    R = gla_round(half, h)
                    pe.wait_ge(evac[(HEAD_TILES * h + 2 + j) % DBANKS].sem, left(half, HEAD_TILES * h + 2 + j))
                    if h == 0 and j == 0:
                        pe.wait_ge(fin_act.sem, fin_act.at(half - 1, "c"))
                    if j == 0:
                        pe.wait_ge(v_copy.sem, v_copy.at(R - 1, "t", 1))
                    else:
                        pe.wait_ge(v_copy.sem, v_copy.at(R, "t", 0))
                    transposes(by_tt[3], lambda b: vT[:, b * P:(b + 1) * P]).then_inc(v_pe.sem, 1)

                def gla_slot(g, s):
                    R = gla_round(half, g)
                    if s == 0:
                        pe.wait_ge(evac[(HEAD_TILES * g + 5) % DBANKS].sem, left(half, HEAD_TILES * g + 5))
                        pe.wait_ge(ga_act.sem, ga_act.at(R - 1, "o"))
                        transposes(by_tt[4], lambda b: k_end[:, b * P:(b + 1) * P]).then_inc(ga_pe.sem, 1)
                        for b in range(TT):
                            c = slice(b * P, (b + 1) * P)
                            last = t_.matmul(by_tt[5][:, b], k_dec[:, c], q_dec[:, c], start=True, stop=True)
                        last.then_inc(ga_pe.sem, 1)
                    if s == 1 or s == 3:
                        if s == 1:
                            pe.wait_ge(ga_dve.sem, ga_dve.at(R, "ke"))
                            pe.wait_ge(v_copy.sem, v_copy.at(R, "t", 1))
                            pe.wait_ge(ga_lo.sem, ga_lo.at(R - 1, "lo"))
                        else:
                            pe.wait_ge(ga_dve.sem, ga_dve.at(R, "st", 3))
                        for i in ((0, 1) if s == 1 else (2, 3)):
                            for c in (2 * i, 2 * i + 1):
                                r = slice(c % 2 * CHUNK, c % 2 * CHUNK + CHUNK)
                                last = t_.matmul(by_dv[6 + c % 2][:, i % 2], ke_tok[r, i], v_tok[r, i], start=True,
                                                 stop=True)
                            last.then_inc(ga_pe.sem, 1)
                    if s == 5 or s == 6:
                        pe.wait_ge(ga_dve.sem, ga_dve.at(R, "mask"))
                        pe.wait_ge(ga_dve.sem, ga_dve.at(R, "st", NCH - 2))
                        for b in ((0, 1) if s == 5 else (2, 3)):
                            o = by_dv[4 + b // 2][:, b % 2]
                            t_.matmul(o, masked[:, b], v_tok[:, b], start=True, stop=False, skip_group_check=True)
                            for c in (2 * b, 2 * b + 1):
                                r = slice(c % 2 * CHUNK, c % 2 * CHUNK + CHUNK)
                                last = t_.matmul(o[r], q_dec[:, c * CHUNK:(c + 1) * CHUNK], state[:, c],
                                                 start=False, stop=True, skip_group_check=True)
                        last.then_inc(ga_pe.sem, 1)
                    if s == 10:
                        pe.wait_ge(ga_act.sem, ga_act.at(R, "o"))
                        pe.wait_ge(ga_dve.sem, ga_dve.at(R, "st"))
                        for j in range(2):
                            transposes(by_tt[6 + j],
                                       lambda b: o_tok[:, b, j * P:(j + 1) * P]).then_inc(ga_pe.sem, 1)

                for h in range(GLA_HEADS + 1):
                    for t in range(HEAD_TILES):
                        def slot(s):
                            if h > 0:
                                gla_slot(h - 1, s)
                            if h < GLA_HEADS and s == 2:
                                alpha(h)
                            if h < GLA_HEADS and s in (6, 8):
                                v_turn(h, (s - 6) // 2)
                        dense(half, HEAD_TILES * h + t, act_x, lambda: slot(2 * t))
                        slot(2 * t + 1)
                for c in range(HEAD_TILES, KB):
                    dense(half, N_GATE_A + c, act_x)
                pe.wait_ge(ga_lo.sem, ga_lo.at(gla_round(half, GLA_HEADS - 1), "lo"))
                for c in range(KB):
                    dense(half, N_BRANCH_A + c, act_o)

                def qk_sum(p, i):
                    R = qk_round(half, p, i)
                    pe.wait_ge(sn_act.sem, sn_act.at(R, "sq"))
                    if i == 1:
                        pe.wait_ge(sv_lo.sem, sv_lo.at(swa_round(half, p), "keep"))
                    elif i > 0 or p > 0:
                        pe.wait_ge(sn_lo.sem, sn_lo.at(R - 1, "l"))
                    t_.matmul(bank[2][:], ones_hd[:], sq_ring[:, 0], start=True, stop=True).then_inc(sn_pe.sem, 1)

                def swa_slot(p, s):
                    if s < UNITS:
                        b, jj = s // 2, s % 2
                        R = unit_round(half, p, s)
                        pe.wait_ge(sn_lo.sem, sn_lo.at(qk_round(half, p, 2 + 2 * jj), "l"))
                        pe.wait_ge(sm_dve.sem, sm_dve.at(R - 1, "ttr"))
                        for e in range(2):
                            for r in range(2):
                                rows_ = slice(r * HD, r * HD + HD)
                                o = bank[3 + r][:, e * 2 * P:(e + 1) * 2 * P]
                                qh, ql = (w[rows_, 4 * p + 2 * jj + e, b * P:(b + 1) * P] for w in act_o)
                                kh, kl = (w[rows_, p, b * P:(b + 2) * P] for w in k_win)
                                t_.matmul(o, qh, kh, start=True, stop=False)
                                t_.matmul(o, ql, kh, start=False, stop=False)
                                last = t_.matmul(o, qh, kl, start=False, stop=True)
                        last.then_inc(sc_pe.sem, 1)
                    if 3 <= s <= UNITS + 2:
                        u = s - 3
                        b, jj = u // 2, u % 2
                        R = unit_round(half, p, u)
                        pe.wait_ge(pt_lo.sem, pt_lo.at(R, "l"))
                        if jj == 0:
                            pe.wait_ge(so_lo.sem, so_lo.at(block_round(half, p, b) - 1, "l"))
                            if u == 0:
                                pe.wait_ge(sv_lo.sem, sv_lo.at(swa_round(half, p), "old"))
                        for r in (1, 0):
                            o = bank[7][0:(r + 1) * HD, jj * 2 * P:(jj + 1) * 2 * P]
                            for k in range(2):
                                vh, vl = (w[:, p, b + k, 0:(r + 1) * HD] for w in v_win)
                                t_.matmul(o, vh, probT[0][:, r, k], start=k == 0, stop=False)
                                t_.matmul(o, vl, probT[0][:, r, k], start=False, stop=False)
                                last = t_.matmul(o, vh, probT[1][:, r, k], start=False, stop=k == 1)
                        last.then_inc(pv_pe.sem, 1)
                    if 2 <= s <= UNITS + 1:
                        R = unit_round(half, p, s - 2)
                        pe.wait_ge(dn_dve.sem, dn_dve.at(R, "norm"))
                        for r in range(2):
                            pe.wait_ge(pt_lo.sem, pt_lo.at(R - 1, "l", r))
                            for k in range(2):
                                for e in range(2):
                                    last = t_.transpose(by_tt[5 + r][:, 2 * k + e],
                                                        prob[:, (s - 2) % 2, 2 * r + e, k * P:(k + 1) * P], ident[:])
                            last.then_inc(pt_pe.sem, 1)

                for p in range(PAIRS):
                    for t in range(HEAD_TILES):
                        def middle():
                            if t == 0 and p > 0:
                                qk_sum(p - 1, 4)
                            if t == 1 or t > 2:
                                qk_sum(p, 0 if t == 1 else t - 2)
                            if t == 2:
                                pe.wait_ge(evac[(N_SWA + p * HEAD_TILES + 1) % DBANKS].sem, left(half, N_SWA + p * HEAD_TILES + 1))
                                pe.wait_ge(sk_lo.sem, sk_lo.at(swa_round(half, p), "keep"))
                                transposes(by_tt[2], lambda b: svT[:, b * P:(b + 1) * P]).then_inc(sv_pe.sem, 1)
                            if p > 0 and t > 0:
                                swa_slot(p - 1, 2 * t - 1)
                        dense(half, N_SWA + p * HEAD_TILES + t, act_x, middle)
                        if p > 0:
                            swa_slot(p - 1, 2 * t)
                for c in range(KB):
                    def middle():
                        if c == 0:
                            qk_sum(PAIRS - 1, 4)
                        else:
                            swa_slot(PAIRS - 1, 2 * c - 1)
                    dense(half, N_GATE_B + c, act_x, middle)
                    swa_slot(PAIRS - 1, 2 * c)
                pe.wait_ge(so_lo.sem, so_lo.at(block_round(half, PAIRS - 1, TT - 1), "l"))
                for c in range(KB):
                    dense(half, N_BRANCH_B + c, act_o)
                for c in range(KB):
                    def residual():
                        if c % 4 == 0:
                            pe.wait_ge(res_loaded[c // 4], half * 16 + 16)
                        if c >= 2:
                            pe.wait_ge(res_copy.sem, res_copy.at(half, "c", c - 2))
                        transposes(by_tt[2 + c % 2], lambda b: gate[:, c // 4 * TT + b, c % 4 * P:(c % 4 + 1) * P]
                                   ).then_inc(res_pe.sem, 1)
                    def merged(k):
                        pe.wait_ge(evac[k % DBANKS].sem, left(half, N_BRANCH_B + k))
                    dense(half, N_OUT + c, act_m, residual, ready=merged if c == 0 else None)

                def up(j, n, turn):
                    if n < N_MLP + KB and j == 0:
                        dense(half, n, act_x, turn=turn,
                              ready=lambda k: pe.wait_ge(hm_lo.sem, hm_lo.at(half, "l", k)))
                    else:
                        dense(half, n, act_x, turn=turn)

                def down(c, turn, mid=None):
                    def ready(k):
                        pe.wait_ge(evac[k % DBANKS].sem, left(half, N_MLP + k, turn))
                    dense(half, N_MLP + KB + c, act_o, mid, turn, ready if c == 0 else None)

                for j in range(KB):
                    up(j, N_MLP + j, 0)
                    if j == 0:
                        pe.wait_ge(hm_add.sem, hm_add.at(half, "a"))
                        t_.matmul(bank[6][:], ones[:], sq_sum[:], start=True, stop=True).then_inc(hm_sum.sem, 1)
                with nc.tensor.Fori(0, MLP_TURNS - 1) as turn:
                    for c in range(KB):
                        down(c, turn)
                    for j in range(KB):
                        up(j, N_MLP + 2 * KB + j, turn)

                def final(c):
                    n = N_MLP + KB + c
                    pe.wait_ge(evac[n % DBANKS].sem, left(half, n, MLP_TURNS - 1))
                    if c >= 2:
                        pe.wait_ge(fin_act.sem, fin_act.at(half, "c", c - 2))
                    transposes(by_tt[2 + c % 2], lambda b: resid[:, c, b * P:(b + 1) * P]).then_inc(fin_pe.sem, 1)

                for c in range(KB):
                    down(c, MLP_TURNS - 1, lambda: x_scaled(half + 1, c))
                    if c > 0:
                        final(c - 1)
                final(KB - 1)


def kernel(**inputs):
    import numpy as _np
    import concourse.bacc as _bacc
    from concourse import mybir as _mybir
    from concourse.bass_utils import run_bass_kernel_spmd as _run

    names = ["x", "norm_mix", "w_in", "w_alpha2", "b_alpha", "gla_norm", "swa_q_norm", "swa_k_norm", "swa_sinks",
             "w_branch_gla", "w_branch_swa", "w_out", "norm_mlp", "w_up", "w_down"]
    nc = _bacc.Bacc("TRN2", target_bir_lowering=False, num_devices=1)
    arrays, args = {}, []
    for name in names:
        a = _np.ascontiguousarray(inputs[name])
        arrays[f"in_{name}_dram"] = a
        args.append(nc.dram_tensor(f"in_{name}_dram", a.shape, _mybir.dt.from_np(a.dtype), kind="ExternalInput").ap())
    args.append(nc.dram_tensor("out_0_dram", (1, SEQ, D_MODEL), _mybir.dt.float32, kind="ExternalOutput").ap())
    program(nc, *args)
    r = _run(nc, [arrays], core_ids=[0])
    return r.results[0]["out_0_dram"]
```
